# Optimizing a Trainium2 kernel written in Bass

```python
import jax, jax.numpy as jnp
from jax import lax
import numpy as np

D_MODEL = 1024
BATCH = 1
SEQ = 256
DEPTH = 1
DEC_BATCH = 8
DEC_SEQ = 1
PAST_LEN = 2048
PAGE_SIZE = 128

HEAD_DIM = 64
D_RWKV = D_MODEL
N_HEADS = D_RWKV // HEAD_DIM
D_DECAY_LORA = 64
D_AAA_LORA = 64
D_GATE_LORA = 128
GN_EPS = 64e-5
D_CONV = D_MODEL
CONV_WIDTH = 31
LN_EPS = 1e-5
N_EXPERTS = 64
N_GROUPS = 8
TOPK_GROUPS = 4
TOP_K = 8
D_EXPERT = 256
D_SHARED = 256
ROUTED_SCALE = 2.5
MOE_BLOCK = 256
RMS_EPS = 1e-6

O_R = 0
O_K = O_R + D_RWKV
O_V = O_K + D_RWKV
O_W = O_V + D_RWKV
O_A = O_W + D_DECAY_LORA
O_G = O_A + D_AAA_LORA
C_RWKV = O_G + D_GATE_LORA
O_GLU = C_RWKV
O_MIX = O_GLU + 2 * D_CONV
C_IN = O_MIX + 2 * D_MODEL

kernel_name = 'rwkv7_conformer_conv_moe_hybrid_step'

def _rmsnorm(x, g):
    xf = x.astype(jnp.float32)
    y = xf * lax.rsqrt(jnp.mean(xf * xf, axis=-1, keepdims=True) + RMS_EPS) * g.astype(jnp.float32)
    return y.astype(x.dtype)

def _layernorm(xf, g, b):
    mu = jnp.mean(xf, axis=-1, keepdims=True)
    var = jnp.mean(jnp.square(xf - mu), axis=-1, keepdims=True)
    return (xf - mu) * lax.rsqrt(var + LN_EPS) * g.astype(jnp.float32) + b.astype(jnp.float32)

def _wkv_scan(s0, r, decay, k, v, kk, b):
    def step(S, inp):
        r_t, d_t, k_t, v_t, kk_t, b_t = inp
        sa = jnp.einsum('bhvk,bhk->bhv', S, -kk_t)
        S = S * d_t[:, :, None, :] + sa[..., None] * b_t[:, :, None, :] + v_t[..., None] * k_t[:, :, None, :]
        return S, jnp.einsum('bhvk,bhk->bhv', S, r_t)
    seq = tuple(jnp.moveaxis(t, 1, 0) for t in (r, decay, k, v, kk, b))
    s_new, o = lax.scan(step, s0, seq)
    return s_new, jnp.moveaxis(o, 0, 1)

def _mixers(xn, s_wkv, s_shift, s_conv, p):
    f32 = jnp.float32
    B, T, _ = xn.shape
    z = xn @ p['w_in']
    zr = z[..., :C_RWKV]
    zr_prev0 = (s_shift.astype(xn.dtype) @ p['w_in'][:, :C_RWKV]).astype(zr.dtype)
    zr_prev = jnp.concatenate([zr_prev0[:, None, :], zr[:, :-1]], axis=1)
    zm = (zr + (zr_prev - zr) * p['mu_shift']).astype(f32)
    r = zm[..., O_R:O_K]
    k = zm[..., O_K:O_V]
    v = zm[..., O_V:O_W]
    w_lora = jnp.tanh(zm[..., O_W:O_A]) @ p['w_decay_up'].astype(f32)
    w_log = -jax.nn.softplus(-(p['w0'].astype(f32) + w_lora)) - 0.5
    decay = jnp.exp(-jnp.exp(w_log))
    a = jax.nn.sigmoid(p['a0'].astype(f32) + zm[..., O_A:O_G] @ p['a_up'].astype(f32))
    g = jax.nn.sigmoid(zm[..., O_G:C_RWKV]) @ p['g_up'].astype(f32)
    hd = lambda t: t.reshape(B, T, N_HEADS, HEAD_DIM)
    kk = hd(k * p['k_k'].astype(f32))
    kk = kk / jnp.maximum(jnp.sqrt(jnp.sum(kk * kk, axis=-1, keepdims=True)), 1e-12)
    k = k * (1.0 + (a - 1.0) * p['k_a'].astype(f32))
    r, k, v, a, decay = hd(r), hd(k), hd(v), hd(a), hd(decay)
    s_wkv_new, o = _wkv_scan(s_wkv.astype(f32), r, decay, k, v, kk, kk * a)
    mu = jnp.mean(o, axis=-1, keepdims=True)
    var = jnp.mean(jnp.square(o - mu), axis=-1, keepdims=True)
    o = ((o - mu) * lax.rsqrt(var + GN_EPS)).reshape(B, T, D_RWKV)
    o = o * p['gn_g'].astype(f32) + p['gn_b'].astype(f32)
    bonus = (jnp.sum(r * k * p['r_k'].astype(f32), axis=-1, keepdims=True) * v).reshape(B, T, D_RWKV)
    out_a = (o + bonus) * g
    glu = z[..., O_GLU:O_MIX]
    u = glu[..., :D_CONV] * jax.nn.sigmoid(glu[..., D_CONV:])
    u_full = jnp.concatenate([s_conv.astype(u.dtype), u], axis=1)
    c = lax.conv_general_dilated(u_full, p['conv_w'][:, None, :].astype(u.dtype),
                                 window_strides=(1,), padding='VALID',
                                 dimension_numbers=('NWC', 'WIO', 'NWC'),
                                 feature_group_count=D_CONV)
    c = c.astype(f32) + p['conv_b'].astype(f32)
    out_b = jax.nn.silu(_layernorm(c, p['cln_g'], p['cln_b']))
    gates = jax.nn.sigmoid(z[..., O_MIX:].astype(f32))
    merged = gates[..., :D_MODEL] * out_a + gates[..., D_MODEL:] * out_b
    y = merged.astype(xn.dtype) @ p['w_out']
    return y, s_wkv_new, xn[:, -1], u_full[:, -(CONV_WIDTH - 1):]

def _moe(x, p):
    B, T, D = x.shape
    xf = x.reshape(B * T, D)
    n = xf.shape[0]
    scores = jax.nn.sigmoid(xf.astype(jnp.float32) @ p['w_router'].astype(jnp.float32))
    biased = scores + p['e_bias'].astype(jnp.float32)
    grp = biased.reshape(n, N_GROUPS, N_EXPERTS // N_GROUPS)
    grp_score = jnp.sum(lax.top_k(grp, 2)[0], axis=-1)
    _, gidx = lax.top_k(grp_score, TOPK_GROUPS)
    gmask = jnp.sum(jax.nn.one_hot(gidx, N_GROUPS, dtype=jnp.float32), axis=1) > 0
    emask = jnp.repeat(gmask, N_EXPERTS // N_GROUPS, axis=1)
    _, eidx = lax.top_k(jnp.where(emask, biased, -jnp.inf), TOP_K)
    wsel = jnp.take_along_axis(scores, eidx, axis=-1)
    wsel = wsel / jnp.sum(wsel, axis=-1, keepdims=True) * ROUTED_SCALE
    gate = jnp.sum(jax.nn.one_hot(eidx, N_EXPERTS, dtype=jnp.float32) * wsel[..., None], axis=1)
    n_pad = (-n) % MOE_BLOCK
    xp = jnp.pad(xf, ((0, n_pad), (0, 0))).reshape(-1, MOE_BLOCK, D)
    gp = jnp.pad(gate, ((0, n_pad), (0, 0))).reshape(-1, MOE_BLOCK, N_EXPERTS)
    w_gate, w_up, w_down = p['w_gate'], p['w_up'], p['w_down']

    def expert_block(args):
        xb, gb = args
        h = jax.nn.silu(jnp.einsum('td,edf->tef', xb, w_gate)) * jnp.einsum('td,edf->tef', xb, w_up)
        h = h * gb[..., None].astype(h.dtype)
        return jnp.einsum('tef,efd->td', h, w_down)

    routed = lax.map(expert_block, (xp, gp)).reshape(-1, D)[:n]
    shared = (jax.nn.silu(xf @ p['ws_gate']) * (xf @ p['ws_up'])) @ p['ws_down']
    return (routed + shared).astype(x.dtype).reshape(B, T, D)

def _layer(x, s_wkv, s_shift, s_conv, p):
    mix, s_wkv_new, s_shift_new, s_conv_new = _mixers(_rmsnorm(x, p['norm1_g']), s_wkv, s_shift, s_conv, p)
    h = x + mix
    y = h + _moe(_rmsnorm(h, p['norm2_g']), p)
    return y, s_wkv_new, s_shift_new, s_conv_new

def setup_inputs(seed: int = 0) -> dict:
    key = jax.random.key(seed)
    ks = jax.random.split(key, 40)
    f32 = jnp.float32
    nrm = lambda k, shape, s: jax.random.normal(k, shape, f32) * s
    L = DEPTH
    return {
        'x_prompt': nrm(ks[0], (BATCH, SEQ, D_MODEL), 1.0),
        'x_sample': nrm(ks[1], (DEC_BATCH, DEC_SEQ, D_MODEL), 1.0),
        'state_wkv': nrm(ks[2], (L, DEC_BATCH, N_HEADS, HEAD_DIM, HEAD_DIM), 0.3),
        'state_shift': nrm(ks[3], (L, DEC_BATCH, D_MODEL), 1.0),
        'state_conv': nrm(ks[4], (L, DEC_BATCH, CONV_WIDTH - 1, D_CONV), 0.5),
        'norm1_g': 1.0 + nrm(ks[5], (L, D_MODEL), 0.02),
        'w_in': nrm(ks[6], (L, D_MODEL, C_IN), D_MODEL ** -0.5),
        'mu_shift': jax.random.uniform(ks[7], (L, C_RWKV), f32),
        'w0': nrm(ks[8], (L, D_RWKV), 1.0),
        'w_decay_up': nrm(ks[9], (L, D_DECAY_LORA, D_RWKV), 0.5 * D_DECAY_LORA ** -0.5),
        'a0': nrm(ks[10], (L, D_RWKV), 0.5),
        'a_up': nrm(ks[11], (L, D_AAA_LORA, D_RWKV), 0.5 * D_AAA_LORA ** -0.5),
        'g_up': nrm(ks[12], (L, D_GATE_LORA, D_RWKV), D_GATE_LORA ** -0.5),
        'k_k': 0.85 + nrm(ks[13], (L, D_RWKV), 0.05),
        'k_a': 1.0 + nrm(ks[14], (L, D_RWKV), 0.05),
        'r_k': nrm(ks[15], (L, N_HEADS, HEAD_DIM), 0.1),
        'gn_g': 1.0 + nrm(ks[16], (L, D_RWKV), 0.02),
        'gn_b': nrm(ks[17], (L, D_RWKV), 0.02),
        'conv_w': nrm(ks[18], (L, CONV_WIDTH, D_CONV), CONV_WIDTH ** -0.5),
        'conv_b': nrm(ks[19], (L, D_CONV), 0.02),
        'cln_g': 1.0 + nrm(ks[20], (L, D_CONV), 0.02),
        'cln_b': nrm(ks[21], (L, D_CONV), 0.02),
        'w_out': nrm(ks[22], (L, D_MODEL, D_MODEL), 0.5 * D_MODEL ** -0.5),
        'norm2_g': 1.0 + nrm(ks[23], (L, D_MODEL), 0.02),
        'w_router': nrm(ks[24], (L, D_MODEL, N_EXPERTS), D_MODEL ** -0.5),
        'e_bias': nrm(ks[25], (L, N_EXPERTS), 0.01),
        'w_gate': nrm(ks[26], (L, N_EXPERTS, D_MODEL, D_EXPERT), D_MODEL ** -0.5),
        'w_up': nrm(ks[27], (L, N_EXPERTS, D_MODEL, D_EXPERT), D_MODEL ** -0.5),
        'w_down': nrm(ks[28], (L, N_EXPERTS, D_EXPERT, D_MODEL), D_EXPERT ** -0.5),
        'ws_gate': nrm(ks[29], (L, D_MODEL, D_SHARED), D_MODEL ** -0.5),
        'ws_up': nrm(ks[30], (L, D_MODEL, D_SHARED), D_MODEL ** -0.5),
        'ws_down': nrm(ks[31], (L, D_SHARED, D_MODEL), D_SHARED ** -0.5),
        'normf_g': 1.0 + nrm(ks[32], (D_MODEL,), 0.02),
    }

def reference(x_prompt, x_sample, state_wkv, state_shift, state_conv, norm1_g, w_in, mu_shift, w0,
              w_decay_up, a0, a_up, g_up, k_k, k_a, r_k, gn_g, gn_b, conv_w, conv_b, cln_g, cln_b,
              w_out, norm2_g, w_router, e_bias, w_gate, w_up, w_down, ws_gate, ws_up, ws_down, normf_g):
    hp, hs = x_prompt, x_sample
    wkv_p, shift_p, conv_p, wkv_s, shift_s, conv_s = [], [], [], [], [], []
    for l in range(DEPTH):
        p = {'norm1_g': norm1_g[l], 'w_in': w_in[l], 'mu_shift': mu_shift[l], 'w0': w0[l],
             'w_decay_up': w_decay_up[l], 'a0': a0[l], 'a_up': a_up[l], 'g_up': g_up[l],
             'k_k': k_k[l], 'k_a': k_a[l], 'r_k': r_k[l], 'gn_g': gn_g[l], 'gn_b': gn_b[l],
             'conv_w': conv_w[l], 'conv_b': conv_b[l], 'cln_g': cln_g[l], 'cln_b': cln_b[l],
             'w_out': w_out[l], 'norm2_g': norm2_g[l], 'w_router': w_router[l], 'e_bias': e_bias[l],
             'w_gate': w_gate[l], 'w_up': w_up[l], 'w_down': w_down[l],
             'ws_gate': ws_gate[l], 'ws_up': ws_up[l], 'ws_down': ws_down[l]}
        z_wkv = jnp.zeros((hp.shape[0], N_HEADS, HEAD_DIM, HEAD_DIM), jnp.float32)
        z_shift = jnp.zeros((hp.shape[0], D_MODEL), hp.dtype)
        z_conv = jnp.zeros((hp.shape[0], CONV_WIDTH - 1, D_CONV), hp.dtype)
        hp, a1, a2, a3 = _layer(hp, z_wkv, z_shift, z_conv, p)
        hs, b1, b2, b3 = _layer(hs, state_wkv[l], state_shift[l], state_conv[l], p)
        wkv_p.append(a1.astype(state_wkv.dtype))
        shift_p.append(a2.astype(state_shift.dtype))
        conv_p.append(a3.astype(state_conv.dtype))
        wkv_s.append(b1.astype(state_wkv.dtype))
        shift_s.append(b2.astype(state_shift.dtype))
        conv_s.append(b3.astype(state_conv.dtype))
    y_prompt = _rmsnorm(hp, normf_g)
    y_sample = _rmsnorm(hs, normf_g)
    return (y_prompt, y_sample, jnp.stack(wkv_p), jnp.stack(shift_p), jnp.stack(conv_p),
            jnp.stack(wkv_s), jnp.stack(shift_s), jnp.stack(conv_s))


_drawn_inputs = setup_inputs


def setup_inputs(seed=0):
    import zlib

    import numpy as np

    out = dict(_drawn_inputs(seed))
    spreads = {}
    factors = {'k_k': 3.887, 'gn_g': 2.729, 'cln_g': 3.01, 'cln_b': 2.95, 'normf_g': 2.719}
    for name, (base, spread) in spreads.items():
        noise = np.random.default_rng([zlib.crc32(name.encode()), seed]).standard_normal(out[name].shape)
        drawn = base * np.exp(spread * noise) if base else spread * noise
        out[name] = __import__('jax').numpy.asarray(drawn.astype(out[name].dtype))
    for name, factor in factors.items():
        out[name] = (out[name] * factor).astype(out[name].dtype)
    return out
```

```python
import numpy as np
from contextlib import ExitStack

import concourse.bass as bass
from concourse import mybir

F32 = mybir.dt.float32
U32 = mybir.dt.uint32
I32 = mybir.dt.int32
ALU = mybir.AluOpType
ACT = mybir.ActivationFunctionType
AX = mybir.AxisListType

D = 1024
NP = 256
NS = 8
NT = NP + NS
NCOL = NP + 2 * NS
KT = D // 128
NG = 4
CH = 64
NCH = NP // CH
NU = 2 * NCH
CW = 31
NE, FE = 64, 256
SLOTS = 64
MAXPASS = (NT + SLOTS - 1) // SLOTS
GN_EPS, LN_EPS, RMS_EPS = 64e-5, 1e-5, 1e-6
EXP_M05 = float(np.exp(-0.5))
LEVELS = (2, 4, 8, 16, 32)

C_R, C_K, C_V, C_LORA = 0, D, 2 * D, 3 * D
C_GLU_A = 3 * D + 256
C_GLU_B = C_GLU_A + D
C_MIX_A = C_GLU_A + 2 * D
C_MIX_B = C_MIX_A + D
GROUP_SECTIONS = (C_R, C_K, C_V, C_GLU_B, C_GLU_A, C_MIX_A, C_MIX_B)
NSEC = len(GROUP_SECTIONS)
NZ = 2 * NSEC

VECS = ('mu_shift', 'w0', 'a0', 'k_k', 'k_a', 'r_k', 'gn_g', 'gn_b', 'conv_b', 'cln_g', 'cln_b')
VROWS = {'mu_shift': 26}
VOFF, _n = {}, 0
for _v in VECS:
    VOFF[_v] = _n
    _n += VROWS.get(_v, KT)
NVEC = _n


def constants():
    p = np.arange(128)
    t = p % 64
    parts = {}
    parts['ident'] = np.eye(128)
    parts['same_head'] = (p[:, None] // 64 == p[None, :] // 64)
    parts['ones'] = np.ones((128, 128))
    s = np.arange(64)
    parts['eye_st'] = (t[:, None] == s[None, :])
    parts['upper'] = np.concatenate([t[:, None] < s[None, :], t[:, None] <= s[None, :]], 1)
    low1 = (t[:, None] // 2 == s[None, :] // 2) & (t[:, None] % 2 == 1) & (s[None, :] % 2 == 0)
    up1 = (t[:, None] // 2 == s[None, :] // 2) & (t[:, None] % 2 == 0) & (s[None, :] % 2 == 1)
    parts['pair_low'], parts['pair_up'] = low1, up1
    for m in LEVELS:
        parts[f'level{m}'] = ((t[:, None] // (2 * m) == s[None, :] // (2 * m))
                              & (t[:, None] // m % 2 == 1) & (s[None, :] // m % 2 == 0))
    parts['before'] = p[:, None] < p[None, :]
    g = np.arange(8)
    parts['lower_group'] = np.tile((g[None, :] < g[:, None]).reshape(1, 64), (128, 1))
    parts['slot'] = np.tile(np.arange(SLOTS * MAXPASS)[None, :], (128, 1))
    parts['dump'] = (NT + p)[:, None]
    parts['token'] = p[:, None] + 128 * np.arange(3)[None, :]
    tok = p[:, None] + 128 * np.arange(3)[None, :]
    parts['row_valid'] = tok < NT
    parts['row_pad'] = tok >= NT
    parts['gn_eps'] = np.full((128, 1), GN_EPS)
    parts['ln_eps'] = np.full((128, 1), LN_EPS)
    parts['rms_eps'] = np.full((128, 1), RMS_EPS)
    off, cols = {}, 0
    for k, v in parts.items():
        off[k] = (cols, cols + v.shape[1])
        cols += v.shape[1]
    return np.concatenate([np.asarray(v, np.float32) for v in parts.values()], 1), off


CONST_ARRAY, CONST_OFF = constants()
NCONST = CONST_ARRAY.shape[1]


def layer_step(nc, A, out, stop=9):
    ctx = ExitStack()
    with ctx:
        def sb(name, shape, dt=F32):
            return ctx.enter_context(nc.sbuf_tensor(name, shape, dt))

        def sem(name):
            return ctx.enter_context(nc.semaphore(name))

        class Arena:
            def __init__(self, base, start, end):
                self.base, self.at, self.end = base, start, end

            def take(self, *dims):
                n = int(np.prod(dims))
                ap = self.base[:, self.at:self.at + n]
                self.at += n
                assert self.at <= self.end, (self.at, self.end)
                names = 'abcd'[:len(dims)]
                if len(dims) > 1:
                    ap = ap.rearrange(f"p ({' '.join(names)}) -> p {' '.join(names)}",
                                      **{names[i]: dims[i] for i in range(len(dims))})
                return ap

        TOTAL = 53200
        big = sb("big", [128, TOTAL])
        keep = Arena(big, 0, TOTAL)
        const = keep.take(NCONST)
        K = {k: const[:, a:b] for k, (a, b) in CONST_OFF.items()}
        ident = K['ident']
        xrow = keep.take(3, D)
        grow = keep.take(D)
        VC = keep.take(NVEC)
        omu = keep.take(26)
        oka = keep.take(KT)
        CWT = keep.take(KT, CW)
        stat = keep.take(16)
        front0 = keep.at
        F = Arena(big, front0, TOTAL)
        C = F.take(KT, NCOL)
        GB = F.take(KT, NCOL)
        MA = F.take(KT, NCOL)
        after_groups0 = F.at
        xT = F.take(KT, NCOL)
        NW = 2
        wring = [F.take(KT, 256) for _ in range(NW)]
        wlora = F.take(D)
        wgate = F.take(D)
        TW = F.take(NCOL)
        SG = F.take(NCOL)
        zs = F.take(2, NCOL + 1)
        LZ = F.take(3, 2, NCOL)
        DC = F.take(2, NCOL)
        AA = F.take(2, NCOL)
        G = F.take(2, NCOL)
        SB = F.take(2, NCOL)
        GA = F.take(2, NCOL)
        KK = F.take(2, NCOL)
        SQ = F.take(2, NCOL)
        INV = F.take(2, NCOL)
        O = F.take(2, NCOL)
        PP = F.take(2, NCH, CH + 1)
        IP = F.take(2, NCH, CH)
        UU = F.take(2, CW - 1 + NCOL)
        AR = F.take(NU, 2, CH)
        BP = F.take(NU, CH)
        KP = F.take(NU, CH)
        a_bd, b_bd, k_bd = (F.take(NU, 128) for _ in range(3))
        X1 = F.take(NU, 2, CH)
        X2 = F.take(NU, 2, CH)
        LT_bd, AK_bd = (F.take(NU, 128) for _ in range(2))
        T_st, TT_st, Y_st = (F.take(NU, CH) for _ in range(3))
        TT_bd, Y_bd = (F.take(NU, 128) for _ in range(2))
        BT_bd, KTok_bd, V_bd = (F.take(NU, 128) for _ in range(3))
        V_st = F.take(NU, CH)
        Z_st, U_st, S_st = (F.take(2, CH) for _ in range(3))
        U_bd, S_bd, SO = (F.take(2, 128) for _ in range(3))
        QS = F.take(2, 6, NS)
        QR = F.take(256)
        QV = F.take(6, CH)
        SM = F.take(16, CH)
        SMT = F.take(16, CH)
        SA = F.take(16)
        OS = F.take(16)
        OR = F.take(256)
        SCR = F.take(2, 256)
        SCB = F.take(2, NS, CW)
        SCT = F.take(NS, CW)
        UR = F.take(256)
        QVV = F.take(16)
        SCR8 = F.take(NS)
        zero1 = F.take(1)
        VD = SMT.rearrange("p a b -> p (a b)").rearrange("p (u r n) -> p u r n", u=NU, r=2)
        INV2 = O
        flat = lambda x: x.rearrange({3: "p a b -> p (a b)", 4: "p a b c -> p (a b c)"}[len(x.shape)])
        junk, shiftrows, convrows = flat(BT_bd), flat(AR), flat(X1)
        vecrows = flat(X2)[:, 0:128]
        P2 = Arena(big, after_groups0, TOTAL)
        w_out_sb = P2.take(KT, D)
        CD = P2.take(KT, NCOL)
        CS = P2.take(KT, NCOL)
        lnr = P2.take(NCOL)
        hrow_x = P2.take(3, D)

        qd = [nc.dram_tensor(f"qd{g}", (48, 256), F32).ap() for g in range(NG)]
        od = [nc.dram_tensor(f"od{g}", (128, 16), F32).ap() for g in range(NG)]
        ps = [ctx.enter_context(nc.psum_tensor(f"bank{i}", [128, 512], F32)) for i in range(8)]
        ZP, B = ps[0:2], ps[2:8]

        names = """
          small_in consts_in x_in vec_in lora_in wout_in hx_in sst_in qv_in os_in dve_chain act_chain xn_ready
          xt_mm xt_ready vec_mm vec_ready xstd_ready zt_mm z_free_dve z_free_act zs_ready lora_ready lora_mm
          lora_free sq_ready ss_mm root_ready dec_ready plain_ready pbd_ready a_mm lmask_ready lbd_ready tr_mm
          tr_free y_mm y_ready ybd_act ybd_pool t_mm tt_mm t_ready tt_ready ttbd_act ttbd_pool zq_mm zq_ready
          u_mm ust_ready ubd_ready o_mm o_ready s_mm s_ready sbd_ready state_zero state_out qs_ready os_ready
          conv_out samp_out gm_mm gd_ready gsq_ready gv_mm gstd_ready bo_in bo_mm ma_ready shift_out
          zero_ready c_ready cm_mm cd_ready csq_ready cv_mm cstd_ready cs_sig cn_ready merged_ready wo_mm
          vd_ready qv_sent tap sm_ready bd_zero od_out
        """.split()
        S = {n: sem(n) for n in names}
        win_in = [sem(f"win_in{i}") for i in range(NW)]
        scr_in = sem("scr_in")
        globals_ = locals()

        block = ctx.enter_context(nc.Block())

        def counted(eng):
            cnt = {}

            def note(ins, name):
                cnt[name] = cnt.get(name, 0) + 1
                ins.then_inc(S[name], 1)

            def link(ins, name):
                note(ins, name)
                eng.wait_ge(S[name], cnt[name])
            return note, link

        def settle(eng):
            eng.sem_inc(S['passed'], 1)

        def wait(eng, name, k):
            if k > 0:
                eng.wait_ge(S[name], k)

        def z_kind(n):
            if n == 0:
                return 'dve'
            if n == 1:
                return 'dve'
            i = (n - 2) % NZ
            return 'act' if i in (6, 7) or i >= 10 else 'dve'

        def z_wait_free(eng, n):
            if n >= 2:
                kind = z_kind(n - 2)
                eng.wait_ge(S[f'z_free_{kind}'], sum(z_kind(m) == kind for m in range(n - 1)))

        vcol = lambda name, j: VC[:, VOFF[name] + j:VOFF[name] + j + 1]
        mucol = lambda i: VC[:, VOFF['mu_shift'] + i:VOFF['mu_shift'] + i + 1]
        w_in = A['w_in'][0].rearrange("(k p) c -> p k c", p=128)
        halves = ((0, 64), (64, 128))

        xg = nc.dram_tensor("xg", (NT + 128, D), F32).ap()
        yd = nc.dram_tensor("yd", (NT + 128, D), F32).ap()
        NSLOT = 4
        ring0 = TOTAL - NSLOT * 3 * 2048
        assert P2.at <= ring0, (P2.at, ring0)
        E = Arena(big, front0, ring0)
        x2p = E.take(3, D)
        x2T = E.take(KT, NT)
        hsh = E.take(2, NT)
        sgs = E.take(2, NT)
        wr = E.take(KT, NE)
        ebias = E.take(NE)
        sc, bi, bm, rp, MK = (E.take(3, NE) for _ in range(5))
        m8 = E.take(24, 8)
        gs, gm, gpen = (E.take(3, 8) for _ in range(3))
        G1, G2 = E.take(3, 8, 8), E.take(3, 8, 8)
        m8b = E.take(3, 8)
        den = E.take(3)
        NEP = NE + 4
        RT = E.take(3, NEP, 3)
        posm = E.take(3, NEP)
        cntf, cnti = E.take(1), E.take(1).bitcast(I32)
        ndump = E.take(1)
        OH = [E.take(3, SLOTS) for _ in range(2)]
        idxt = E.take(4)
        idxf = E.take(4)
        idxu = E.take(4).bitcast(U32)
        gts = E.take(4)
        xe = [E.take(D) for _ in range(2)]
        xeT = [E.take(KT, SLOTS) for _ in range(2)]
        hsg = E.take(2 * SLOTS)
        hT = [E.take(2, SLOTS) for _ in range(2)]
        ye = [E.take(D) for _ in range(2)]
        zrow = E.take(D)
        slot_w = []
        for i in range(NSLOT):
            W_ = Arena(big, ring0 + i * 6144, ring0 + (i + 1) * 6144)
            slot_w.append((W_.take(KT, FE), W_.take(KT, FE), W_.take(2, D)))
        ps_idx, ps_x = ps[0], ps[1]
        ps_h, ps_y = (ps[2], ps[3]), (ps[4], ps[5])

        for n in """wg_in wu_in wd_in""".split():
            for i in range(NSLOT):
                S[f'{n}{i}'] = sem(f'{n}{i}')
        for n in """
          ov_pe ov_act ov_dve ov_ye idx_step sc_ready2 hsg_ready grow_in x2_out dump_out wr_in h2_ready
          h2std_ready x2_ready x2t_mm x2t_ready zrow_ready rt_mm sc_ready mk_ready pos_mm cnt_ready shg_mm
          shs_ready shh_ready shd_mm shy_ready yinit oh_ready idx_mm idx_ready gath0 gath1 xtr_mm xet_ready
          h_mm sig_ready ht_ready yx_mm ye_act ye_dve scat moe_done moe_pe ov_w ov_gath ov_scat fin_in fin_std
          fin_ready fin_out rout_ready passed
        """.split():
            S[n] = sem(n)

        def load_item(sp, part, slot, src):
            dst = slot_w[slot][part]
            if part < 2:
                ap = src.rearrange("(p k) f -> p k f", k=KT)
            else:
                ap = src.rearrange("(j p) d -> p j d", p=128)
            sp.dma_start(dst, ap).then_inc(S[('wg_in', 'wu_in', 'wd_in')[part] + str(slot)], 16)

        def expert_w(part, e):
            name = ('w_gate', 'w_up', 'w_down')[part]
            if isinstance(e, int):
                return A[name][0, e]
            return A[name][0, bass.ds(e, 1)].rearrange("a r c -> (a r) c")

        def moe_sp(sp):
            sp.wait_ge(S['xn_ready'], 3)
            sp.dma_start(grow, A['norm2_g'][0:1, :].partition_broadcast(128)).then_inc(S['grow_in'], 16)
            for part, n in enumerate(('ws_gate', 'ws_up', 'ws_down')):
                load_item(sp, part, 0, A[n][0])
            sp.wait_ge(S['h2_ready'], 6)
            sp.dma_start(wr, A['w_router'][0].rearrange("(p k) e -> p k e", k=KT)).then_inc(S['wr_in'], 16)
            sp.dma_start(ebias, A['e_bias'][0:1, :].partition_broadcast(128)).then_inc(S['wr_in'], 16)
            for e in range(3):
                for part in range(3):
                    load_item(sp, part, e + 1, expert_w(part, e))
            sp.wait_ge(S['x2_ready'], 3)
            sp.dma_start(grow, A['normf_g'].rearrange("(a d) -> a d", a=1).partition_broadcast(128)) \
              .then_inc(S['grow_in'], 16)
            sp.dma_start(xg[0:NP, :].rearrange("(t p) d -> p t d", p=128), x2p[:, 0:2, :]).then_inc(S['x2_out'], 16)
            sp.dma_start(xg[NP:NT, :], x2p[0:NS, 2, :]).then_inc(S['x2_out'], 16)
            sp.wait_ge(S['shg_mm'], 4)
            load_item(sp, 0, 0, expert_w(0, 3))
            load_item(sp, 1, 0, expert_w(1, 3))
            sp.wait_ge(S['shy_ready'], 6)
            sp.dma_start(yd[0:NP, :].rearrange("(t p) d -> p t d", p=128), xrow[:, 0:2, :]).then_inc(S['yinit'], 16)
            sp.dma_start(yd[NP:NT, :], xrow[0:NS, 2, :]).then_inc(S['yinit'], 16)
            load_item(sp, 2, 0, expert_w(2, 3))
            with sp.Fori(1, NE // 4) as i:
                for b in range(4):
                    e = 4 * i + b
                    sp.wait_ge(S['h_mm'], e - 3)
                    load_item(sp, 0, (b + 1) % 4, expert_w(0, e))
                    load_item(sp, 1, (b + 1) % 4, expert_w(1, e))
                    sp.wait_ge(S['yx_mm'], e - 3)
                    load_item(sp, 2, (b + 1) % 4, expert_w(2, e))
            sp.wait_ge(S['cnt_ready'], 1)
            count = sp.value_load(cnti[0:1, 0:1])
            with sp.If(count > SLOTS):
                sp.wait_ge(S['moe_pe'], 1)
                with sp.Fori(0, NE) as e:
                    with sp.If(e > 0):
                        sp.wait_ge(S['ov_pe'], e * (4 * (MAXPASS - 1)))
                        settle(sp)
                    for part, n in enumerate(('w_gate', 'w_up', 'w_down')):
                        ap = expert_w(part, e)
                        ap = (ap.rearrange("(p k) f -> p k f", k=KT) if part < 2
                              else ap.rearrange("(j p) d -> p j d", p=128))
                        sp.dma_start(slot_w[0][part], ap).then_inc(S['ov_w'], 16)
            sp.wait_ge(S['moe_done'], 1)
            sp.dma_start(x2p[:, 0:2, :], yd[0:NP, :].rearrange("(t p) d -> p t d", p=128)).then_inc(S['fin_in'], 16)
            sp.dma_start(x2p[0:NS, 2, :], yd[NP:NT, :]).then_inc(S['fin_in'], 16)
            sp.wait_ge(S['fin_ready'], 3)
            sp.dma_start(out['y_p'][0].rearrange("(t p) d -> p t d", p=128), xrow[:, 0:2, :]).then_inc(S['fin_out'], 16)
            sp.dma_start(out['y_s'][:, 0, :], xrow[0:NS, 2, :]).then_inc(S['fin_out'], 16)
            sp.wait_ge(S['fin_out'], 32)

        def tile_rows(t):
            return 128 if t < 2 else NS

        def moe_pe(pe, note, mm):
            for t in range(3):
                r = tile_rows(t)
                pe.wait_ge(S['x2_ready'], t + 1)
                for k in range(KT):
                    ins = nc.tensor.transpose(B[2 * t + k // 4][:, 128 * (k % 4):128 * (k % 4) + r],
                                              x2p[0:r, t, 128 * k:128 * k + 128], ident[0:r, 0:r])
                    if k % 4 == 3:
                        note(ins, 'x2t_mm')
            pe.wait_ge(S['x2t_ready'], 6)
            pe.wait_ge(S['wr_in'], 32)
            for t in range(3):
                r = tile_rows(t)
                for k in range(KT):
                    ins = mm(B[5][0:r, 64 * t:64 * t + 64], x2T[:, k, 128 * t:128 * t + r], wr[:, k, :],
                             k == 0, k == KT - 1)
            note(ins, 'rt_mm')
            sw = slot_w[0]
            for j in range(2):
                for part in range(2):
                    if j == 0:
                        pe.wait_ge(S[('wg_in0', 'wu_in0')[part]], 16)
                    for k in range(KT):
                        ins = mm(ps[2 * part + j][:, 0:NT], sw[part][:, k, 128 * j:128 * j + 128], x2T[:, k, :],
                                 k == 0, k == KT - 1)
                    note(ins, 'shg_mm')
            pe.wait_ge(S['mk_ready'], 1)
            for t in range(3):
                for s in range(t + 1):
                    ins = mm(ps[7][:, 64 * t:64 * t + 64], K['before'] if s == t else K['ones'], MK[:, s, :],
                             s == 0, s == t)
            for s in range(3):
                ins = mm(ps[7][:, 192:256], K['ones'], MK[:, s, :], s == 0, s == 2)
            note(ins, 'pos_mm')
            pe.wait_ge(S['shh_ready'], 2)
            pe.wait_ge(S['wd_in0'], 16)
            for n, (t, h) in enumerate((t, h) for t in range(3) for h in range(2)):
                r = tile_rows(t)
                bank = ps[(4, 5, 6, 1, 2, 3)[n]]
                for j in range(2):
                    ins = mm(bank[0:r, :], hsh[:, j, 128 * t:128 * t + r], sw[2][:, j, 512 * h:512 * h + 512],
                             j == 0, j == 1)
                note(ins, 'shd_mm')

            pe.wait_ge(S['rout_ready'], 1)
            pe.wait_ge(S['shy_ready'], 6)

            def index(e, b):
                pe.wait_ge(S['oh_ready'], e + 1)
                if not (isinstance(e, int) and e < 1):
                    pe.wait_ge(S['idx_ready'], e)
                settle(pe)
                for t in range(3):
                    rhs = (RT[:, t, e, :] if isinstance(e, int)
                           else RT[:, t, bass.ds(e, 1), :].rearrange("p a c -> p (a c)"))
                    ins = mm(ps_idx[0:SLOTS, 0:3], OH[b % 2][:, t, :], rhs, t == 0, t == 2)
                note(ins, 'idx_mm')

            def turn(e, b):
                pe.wait_ge(S[f'gath{b % 2}'], 16 * (e // 2 + 1) if isinstance(e, int) else e * 8 + (16 if b % 2 == 0 else 8))
                if not (isinstance(e, int) and e < 1):
                    pe.wait_ge(S['xet_ready'], e)
                settle(pe)
                for k in range(KT):
                    ins = nc.tensor.transpose(ps_x[:, SLOTS * k:SLOTS * k + SLOTS],
                                              xe[b % 2][0:SLOTS, 128 * k:128 * k + 128], ident[0:SLOTS, 0:SLOTS])
                note(ins, 'xtr_mm')

            def gate_up(e, i, b):
                s = (b + 1) % 4
                turns = i + (2 if b == 3 else 1)
                pe.wait_ge(S['xet_ready'], e + 1)
                if not (isinstance(e, int) and e < 2):
                    pe.wait_ge(S['ht_ready'], e - 1)
                for part in range(2):
                    pe.wait_ge(S[('wg_in', 'wu_in')[part] + str(s)], 16 * turns)
                    for j in range(2):
                        c = SLOTS * (2 * part + j)
                        for k in range(KT):
                            ins = mm(ps_h[b % 2][:, c:c + SLOTS], slot_w[s][part][:, k, 128 * j:128 * j + 128],
                                     xeT[b % 2][:, k, :], k == 0, k == KT - 1)
                note(ins, 'h_mm')

            def down(e, i, b):
                s = (b + 1) % 4
                turns = i + (2 if b == 3 else 1)
                pe.wait_ge(S['ht_ready'], e + 1)
                pe.wait_ge(S[f'wd_in{s}'], 16 * turns)
                if not (isinstance(e, int) and e < 1):
                    pe.wait_ge(S['ye_act'], e)
                    pe.wait_ge(S['ye_dve'], e)
                for h in range(2):
                    for j in range(2):
                        ins = mm(ps_y[h][0:SLOTS, :], hT[b % 2][:, j, :], slot_w[s][2][:, j, 512 * h:512 * h + 512],
                                 j == 0, j == 1)
                note(ins, 'yx_mm')

            def four(i):
                for b in range(4):
                    e = 4 * i + b
                    index(e + 2, b + 2)
                    turn(e + 1, b + 1)
                    gate_up(e, i, b)
                    if b:
                        down(e - 1, i, b - 1)
                    elif not isinstance(i, int):
                        down(e - 1, i - 1, 3)

            index(0, 0)
            index(1, 1)
            turn(0, 0)
            four(0)
            with pe.Fori(1, NE // 4) as i:
                four(i)
            down(NE - 1, NE // 4 - 1, 3)
            pe.wait_ge(S['cnt_ready'], 1)
            count = pe.value_load(cnti[0:1, 0:1])
            with pe.If(count > SLOTS):
                pe.wait_ge(S['ye_act'], NE)
                pe.wait_ge(S['ye_dve'], NE)
                pe.wait_ge(S['yx_mm'], NE)
                mm(ps[6][0:1, 0:1], K['ones'][:, 0:1], K['ones'][:, 0:1]).then_inc(S['moe_pe'], 1)
                with pe.Fori(0, NE) as e:
                    for c in range(1, MAXPASS):
                        n = e * (MAXPASS - 1) + c
                        pe.wait_ge(S['ov_dve'], 6 * n - 5)
                        settle(pe)
                        for t in range(3):
                            ins = mm(ps_idx[0:SLOTS, 0:3], OH[0][:, t, :],
                                     RT[:, t, bass.ds(e, 1), :].rearrange("p a c -> p (a c)"), t == 0, t == 2)
                        ins.then_inc(S['ov_pe'], 1)
                        pe.wait_ge(S['ov_gath'], 16 * n)
                        settle(pe)
                        for k in range(KT):
                            ins = nc.tensor.transpose(ps_x[:, SLOTS * k:SLOTS * k + SLOTS],
                                                      xe[0][0:SLOTS, 128 * k:128 * k + 128], ident[0:SLOTS, 0:SLOTS])
                        ins.then_inc(S['ov_pe'], 1)
                        pe.wait_ge(S['ov_act'], 2 * n - 1)
                        if c == 1:
                            pe.wait_ge(S['ov_w'], 48 * e + 48)
                        for part in range(2):
                            for j in range(2):
                                cc = SLOTS * (2 * part + j)
                                for k in range(KT):
                                    ins = mm(ps_h[0][:, cc:cc + SLOTS], slot_w[0][part][:, k, 128 * j:128 * j + 128],
                                             xeT[0][:, k, :], k == 0, k == KT - 1)
                        ins.then_inc(S['ov_pe'], 1)
                        pe.wait_ge(S['ov_dve'], 6 * n)
                        for h in range(2):
                            for j in range(2):
                                ins = mm(ps_y[h][0:SLOTS, :], hT[0][:, j, :], slot_w[0][2][:, j, 512 * h:512 * h + 512],
                                         j == 0, j == 1)
                        ins.then_inc(S['ov_pe'], 1)

        def moe_act(act, note, link, fn):
            for t in range(3):
                r = tile_rows(t)
                act.wait_ge(S['h2_ready'], 2 * t + 2)
                link(fn(ye[1][0:r, :], xrow[0:r, t, :], ACT.Square, accum_out=stat[0:r, 9 + t:10 + t]), 'act_chain')
                note(fn(stat[0:r, 12 + t:13 + t], stat[0:r, 9 + t:10 + t], ACT.Sqrt, scale=1.0 / D,
                        bias=K['rms_eps'][0:r, :]), 'h2std_ready')
            for t in range(3):
                r = tile_rows(t)
                for h in range(2):
                    act.wait_ge(S['x2t_mm'], 2 * t + h + 1)
                    note(fn(x2T[:, 4 * h:4 * h + 4, 128 * t:128 * t + r],
                            B[2 * t + h][:, :].rearrange("p (k c) -> p k c", k=4)[:, :, 0:r], ACT.Copy), 'x2t_ready')
            act.wait_ge(S['rt_mm'], 1)
            act.wait_ge(S['sc_ready'], 1)
            for t in range(3):
                r = tile_rows(t)
                note(fn(sc[0:r, t, :], B[5][0:r, 64 * t:64 * t + 64], ACT.Sigmoid), 'sc_ready2')
            for j in range(2):
                act.wait_ge(S['shg_mm'], 2 * j + 1)
                note(fn(sgs[:, j, :], ps[j][:, 0:NT], ACT.Sigmoid), 'shs_ready')

            def turned(e, b):
                act.wait_ge(S['xtr_mm'], e + 1)
                if not (isinstance(e, int) and e < 2):
                    act.wait_ge(S['h_mm'], e - 1)
                note(fn(xeT[b % 2].rearrange("p k n -> p (k n)"), ps_x[:, 0:KT * SLOTS], ACT.Copy), 'xet_ready')

            def sigma(e, b):
                act.wait_ge(S['h_mm'], e + 1)
                if not (isinstance(e, int) and e < 1):
                    act.wait_ge(S['ht_ready'], e)
                note(fn(hsg, ps_h[b % 2][:, 0:2 * SLOTS], ACT.Sigmoid), 'sig_ready')

            def weigh(e, b):
                act.wait_ge(S['yx_mm'], e + 1)
                if not (isinstance(e, int) and e < 2):
                    act.wait_ge(S['scat'], 16 * e - 16)
                note(fn(ye[b % 2][0:SLOTS, 0:512], ps_y[0][0:SLOTS, :], ACT.Copy, scale=gts[0:SLOTS, b % 4:b % 4 + 1]),
                     'ye_act')

            def four(i):
                for b in range(4):
                    e = 4 * i + b
                    turned(e + 1, b + 1)
                    sigma(e, b)
                    if b or not isinstance(i, int):
                        weigh(e - 1, b + 3)

            turned(0, 0)
            four(0)
            with act.Fori(1, NE // 4) as i:
                four(i)
            weigh(NE - 1, 3)
            act.wait_ge(S['cnt_ready'], 1)
            count = act.value_load(cnti[0:1, 0:1])
            with act.If(count > SLOTS):
                with act.Fori(0, NE) as e:
                    for c in range(1, MAXPASS):
                        n = e * (MAXPASS - 1) + c
                        act.wait_ge(S['ov_pe'], 4 * n - 2)
                        fn(xeT[0].rearrange("p k n -> p (k n)"), ps_x[:, 0:KT * SLOTS], ACT.Copy).then_inc(S['ov_act'], 1)
                        act.wait_ge(S['ov_pe'], 4 * n - 1)
                        fn(hsg, ps_h[0][:, 0:2 * SLOTS], ACT.Sigmoid).then_inc(S['ov_act'], 1)
                        act.wait_ge(S['ov_pe'], 4 * n)
                        fn(ye[0][0:SLOTS, 0:512], ps_y[0][0:SLOTS, :], ACT.Copy, scale=gts[0:SLOTS, 0:1]) \
                            .then_inc(S['ov_ye'], 1)
            act.wait_ge(S['fin_in'], 32)
            for t in range(3):
                r = tile_rows(t)
                link(fn(ye[0][0:r, :], x2p[0:r, t, :], ACT.Square, accum_out=stat[0:r, t:t + 1]), 'act_chain')
                note(fn(stat[0:r, 3 + t:4 + t], stat[0:r, t:t + 1], ACT.Sqrt, scale=1.0 / D,
                        bias=K['rms_eps'][0:r, :]), 'fin_std')

        def moe_dve(dve, note, link, v):
            M, AD = ALU.mult, ALU.add
            chain = 'dve_chain'
            dve.wait_ge(S['wo_mm'], 1)
            dve.wait_ge(S['hx_in'], 32)
            dve.wait_ge(S['shift_out'], 48)
            for t in range(3):
                r = tile_rows(t)
                for h in range(2):
                    note(v.tensor_tensor(xrow[0:r, t, 512 * h:512 * h + 512], B[2 * t + h][0:r, :],
                                         hrow_x[0:r, t, 512 * h:512 * h + 512], AD), 'h2_ready')
            v.memset(sc, 0.0)
            v.memset(RT[:, :, NE:NEP, 2:3], 0.0)
            v.memset(RT[:, :, :, 1:2], 1.0)
            link(v.memset(posm[:, :, NE:NEP], 1e6), 'sc_ready')
            dve.wait_ge(S['grow_in'], 16)
            dve.wait_ge(S['h2_ready'], 6)
            for t in range(3):
                r = tile_rows(t)
                dve.wait_ge(S['h2std_ready'], t + 1)
                link(v.reciprocal(stat[0:r, 6 + t:7 + t], stat[0:r, 12 + t:13 + t]), chain)
                link(v.scalar_tensor_tensor(
                    out=x2p[0:r, t, :].rearrange("q (k p) -> q p k", k=KT),
                    in0=xrow[0:r, t, :].rearrange("q (p k) -> q p k", k=KT), scalar=stat[0:r, 6 + t:7 + t],
                    in1=grow[0:r, :].rearrange("q (p k) -> q p k", k=KT), op0=M, op1=M), 'x2_ready')
            dve.wait_ge(S['wr_in'], 32)
            dve.wait_ge(S['sc_ready2'], 3)
            link(v.tensor_tensor(bi, sc, ebias.unsqueeze(1).broadcast_to([128, 3, NE]), AD), chain)
            for t in range(3):
                for q in range(8):
                    ins = v.max(out=m8[:, 8 * t + q, :], in_=bi[:, t, 8 * q:8 * q + 8])
            link(ins, chain)
            link(v.tensor_tensor(gs.rearrange("p t g -> p (t g)"), m8[:, :, 0], m8[:, :, 1], AD), chain)
            other = gs.unsqueeze(2).broadcast_to([128, 3, 8, 8])
            own = gs.unsqueeze(3).broadcast_to([128, 3, 8, 8])
            link(v.tensor_tensor(G2, other, own, ALU.is_equal), chain)
            link(v.tensor_tensor(G2.rearrange("p t a b -> p t (a b)"), G2.rearrange("p t a b -> p t (a b)"),
                                 K['lower_group'].unsqueeze(1).broadcast_to([128, 3, 64]), M), chain)
            link(v.tensor_tensor(G1, other, own, ALU.is_gt), chain)
            link(v.tensor_tensor(G1, G1, G2, AD), chain)
            link(v.tensor_reduce(gm, G1, AX.X, AD), chain)
            link(v.tensor_scalar(gm, gm, 3.5, None, ALU.is_lt), chain)
            link(v.tensor_scalar(gpen, gm, 1e30, -1e30, M, AD), chain)
            by_group = lambda x: x.rearrange("p t (g c) -> p t g c", g=8)
            wide = lambda x: x.unsqueeze(3).broadcast_to([128, 3, 8, 8])
            link(v.tensor_tensor(by_group(bm), by_group(bi), wide(gm), M), chain)
            link(v.tensor_tensor(by_group(bm), by_group(bm), wide(gpen), AD), chain)
            for t in range(3):
                link(v.max(out=m8b[:, t, :], in_=bm[:, t, :]), chain)
                link(v.match_replace(out=rp[:, t, :], in_to_replace=m8b[:, t, :], in_values=bm[:, t, :],
                                     imm_value=-3e38), chain)
            link(v.tensor_scalar(MK, rp, -2e38, None, ALU.is_lt), chain)
            link(v.tensor_tensor(MK, MK, K['row_valid'].unsqueeze(2).broadcast_to([128, 3, NE]), M), 'mk_ready')
            link(v.tensor_tensor(rp, sc, MK, M), chain)
            link(v.tensor_reduce(den, rp, AX.X, AD), chain)
            link(v.tensor_tensor(den, den, K['row_pad'], AD), chain)
            link(v.reciprocal(den, den), chain)
            link(v.tensor_scalar(den, den, 2.5, None, M), chain)
            note(v.tensor_tensor(RT[:, :, 0:NE, 2], rp, den.unsqueeze(2).broadcast_to([128, 3, NE]), M), chain)
            note(v.tensor_copy(RT[:, :, :, 0], K['token'].unsqueeze(2).broadcast_to([128, 3, NEP])), chain)
            note(v.tensor_scalar(ndump, K['dump'], -1.0, None, M), chain)
            link(v.tensor_scalar(bm, MK, -1e6, 1e6, M, AD), chain)
            dve.wait_ge(S['pos_mm'], 1)
            link(v.tensor_tensor(posm[:, :, 0:NE], bm, ps[7][:, 0:192].rearrange("p (t e) -> p t e", t=3), AD),
                 'rout_ready')
            link(v.tensor_reduce(cntf, ps[7][:, 192:256], AX.X, ALU.max), chain)
            link(v.tensor_copy(cnti, cntf), 'cnt_ready')

            def onehot(e, b):
                if not (isinstance(e, int) and e < 2):
                    dve.wait_ge(S['idx_mm'], e - 1)
                col = posm[:, :, e:e + 1] if isinstance(e, int) else posm[:, :, bass.ds(e, 1)]
                note(v.tensor_tensor(OH[b % 2], K['slot'][:, 0:SLOTS].unsqueeze(1).broadcast_to([128, 3, SLOTS]),
                                     col.broadcast_to([128, 3, SLOTS]), ALU.is_equal), 'oh_ready')

            def row_index(e, b, out_sem='idx_ready'):
                dve.wait_ge(S['idx_mm'], e + 1)
                if not (isinstance(e, int) and e < 4):
                    dve.wait_ge(S['scat'], 16 * e - 48)
                r, q = SLOTS, b % 4
                note(v.tensor_copy(idxt[0:r, 0:3], ps_idx[0:r, 0:3]), 'idx_step')
                dve.wait_ge(S['idx_step'], 2 * e + 1)
                note(v.tensor_scalar(idxf[0:r, 0:1], idxt[0:r, 1:2], ndump[0:r, :], K['dump'][0:r, :], M, AD), 'idx_step')
                v.tensor_copy(gts[0:r, q:q + 1], idxt[0:r, 2:3])
                dve.wait_ge(S['idx_step'], 2 * e + 2)
                note(v.tensor_tensor(idxu[0:r, q:q + 1], idxf[0:r, 0:1], idxt[0:r, 0:1], AD), out_sem)

            for j in range(2):
                dve.wait_ge(S['shs_ready'], j + 1)
                link(v.tensor_tensor(sgs[:, j, :], sgs[:, j, :], ps[j][:, 0:NT], M), chain)
                dve.wait_ge(S['shg_mm'], 2 * j + 2)
                note(v.tensor_tensor(hsh[:, j, :], sgs[:, j, :], ps[2 + j][:, 0:NT], M), 'shh_ready')
            for n, (t, h) in enumerate((t, h) for t in range(3) for h in range(2)):
                r = tile_rows(t)
                dve.wait_ge(S['shd_mm'], n + 1)
                x = xrow[0:r, t, 512 * h:512 * h + 512]
                note(v.tensor_tensor(x, x, ps[(4, 5, 6, 1, 2, 3)[n]][0:r, :], AD), 'shy_ready')

            def hidden(e, b):
                dve.wait_ge(S['sig_ready'], e + 1)
                if not (isinstance(e, int) and e < 2):
                    dve.wait_ge(S['yx_mm'], e - 1)
                note(v.tensor_tensor(hsg, hsg, ps_h[b % 2][:, 0:2 * SLOTS], M), 'hsg_ready')
                dve.wait_ge(S['hsg_ready'], e + 1)
                note(v.tensor_tensor(hT[b % 2].rearrange("p j n -> p (j n)"), hsg,
                                     ps_h[b % 2][:, 2 * SLOTS:4 * SLOTS], M), 'ht_ready')

            def weigh(e, b):
                dve.wait_ge(S['yx_mm'], e + 1)
                if not (isinstance(e, int) and e < 2):
                    dve.wait_ge(S['scat'], 16 * e - 16)
                note(v.tensor_scalar(ye[b % 2][0:SLOTS, 512:1024], ps_y[1][0:SLOTS, :],
                                     gts[0:SLOTS, b % 4:b % 4 + 1], None, M), 'ye_dve')

            def four(i):
                for b in range(4):
                    e = 4 * i + b
                    row_index(e + 2, b + 2)
                    onehot(e + 3, b + 3)
                    hidden(e, b)
                    if b or not isinstance(i, int):
                        weigh(e - 1, b + 3)

            onehot(0, 0)
            onehot(1, 1)
            row_index(0, 0)
            onehot(2, 2)
            row_index(1, 1)
            four(0)
            with dve.Fori(1, NE // 4) as i:
                four(i)
            weigh(NE - 1, 3)
            count = dve.value_load(cnti[0:1, 0:1])
            with dve.If(count > SLOTS):
                dve.wait_ge(S['scat'], 16 * NE)
                with dve.Fori(0, NE) as e:
                    for c in range(1, MAXPASS):
                        n = e * (MAXPASS - 1) + c
                        v.tensor_tensor(OH[0], K['slot'][:, SLOTS * c:SLOTS * c + SLOTS].unsqueeze(1)
                                        .broadcast_to([128, 3, SLOTS]),
                                        posm[:, :, bass.ds(e, 1)].broadcast_to([128, 3, SLOTS]),
                                        ALU.is_equal).then_inc(S['ov_dve'], 1)
                        dve.wait_ge(S['ov_pe'], 4 * n - 3)
                        r = SLOTS
                        v.tensor_copy(idxt[0:r, 0:3], ps_idx[0:r, 0:3]).then_inc(S['ov_dve'], 1)
                        dve.wait_ge(S['ov_dve'], 6 * n - 4)
                        v.tensor_scalar(idxf[0:r, 0:1], idxt[0:r, 1:2], ndump[0:r, :], K['dump'][0:r, :], M, AD) \
                            .then_inc(S['ov_dve'], 1)
                        v.tensor_copy(gts[0:r, 0:1], idxt[0:r, 2:3])
                        dve.wait_ge(S['ov_dve'], 6 * n - 3)
                        v.tensor_tensor(idxu[0:r, 0:1], idxf[0:r, 0:1], idxt[0:r, 0:1], AD).then_inc(S['ov_dve'], 1)
                        dve.wait_ge(S['ov_act'], 2 * n)
                        v.tensor_tensor(hsg, hsg, ps_h[0][:, 0:2 * SLOTS], M).then_inc(S['ov_dve'], 1)
                        dve.wait_ge(S['ov_dve'], 6 * n - 1)
                        v.tensor_tensor(hT[0].rearrange("p j n -> p (j n)"), hsg, ps_h[0][:, 2 * SLOTS:4 * SLOTS], M) \
                            .then_inc(S['ov_dve'], 1)
                        dve.wait_ge(S['ov_pe'], 4 * n)
                        v.tensor_scalar(ye[0][0:SLOTS, 512:1024], ps_y[1][0:SLOTS, :], gts[0:SLOTS, 0:1], None, M) \
                            .then_inc(S['ov_ye'], 1)
                        dve.wait_ge(S['ov_scat'], 16 * n)
            dve.wait_ge(S['grow_in'], 32)
            dve.wait_ge(S['fin_in'], 32)
            for t in range(3):
                r = tile_rows(t)
                dve.wait_ge(S['fin_std'], t + 1)
                link(v.reciprocal(stat[0:r, 6 + t:7 + t], stat[0:r, 3 + t:4 + t]), chain)
                note(v.scalar_tensor_tensor(out=xrow[0:r, t, :], in0=x2p[0:r, t, :], scalar=stat[0:r, 6 + t:7 + t],
                                            in1=grow[0:r, :], op0=M, op1=M), 'fin_ready')

        def moe_pool(pool, note, link, gp):
            pool.wait_ge(S['h2_ready'], 6)
            link(gp.memset(zrow, 0.0), 'zrow_ready')
            pool.dma_start(xg[NT:NT + 128, :], zrow).then_inc(S['dump_out'], 16)
            pool.dma_start(yd[NT:NT + 128, :], zrow).then_inc(S['dump_out'], 16)
            pool.wait_ge(S['dump_out'], 32)
            pool.wait_ge(S['x2_out'], 32)

            def rows_of(q):
                return bass.IndirectOffsetOnAxis(ap=idxu[0:SLOTS, q:q + 1], axis=0)

            def gather(e, b):
                pool.wait_ge(S['idx_ready'], e + 1)
                if not (isinstance(e, int) and e < 2):
                    pool.wait_ge(S['xtr_mm'], e - 1)
                settle(pool)
                pool.indirect_dma_start(out=xe[b % 2][0:SLOTS, :], out_offset=None, in_=xg, in_offset=rows_of(b % 4)) \
                    .then_inc(S[f'gath{b % 2}'], 16)

            def scatter(e, b):
                pool.wait_ge(S['ye_act'], e + 1)
                pool.wait_ge(S['ye_dve'], e + 1)
                if not (isinstance(e, int) and e < 1):
                    pool.wait_ge(S['scat'], 16 * e)
                settle(pool)
                pool.indirect_dma_start(out=yd, out_offset=rows_of(b % 4), in_=ye[b % 2][0:SLOTS, :],
                                        in_offset=None, compute_op=ALU.add).then_inc(S['scat'], 16)

            def four(i):
                for b in range(4):
                    e = 4 * i + b
                    gather(e + 2, b + 2)
                    if b or not isinstance(i, int):
                        scatter(e - 1, b + 3)

            gather(0, 0)
            gather(1, 1)
            pool.wait_ge(S['yinit'], 32)
            four(0)
            with pool.Fori(1, NE // 4) as i:
                four(i)
            scatter(NE - 1, 3)
            pool.wait_ge(S['scat'], 16 * NE)
            pool.wait_ge(S['gath1'], 16 * (NE // 2 + 1))
            pool.wait_ge(S['cnt_ready'], 1)
            count = pool.value_load(cnti[0:1, 0:1])
            with pool.If(count > SLOTS):
                with pool.Fori(0, NE) as e:
                    for c in range(1, MAXPASS):
                        n = e * (MAXPASS - 1) + c
                        pool.wait_ge(S['ov_dve'], 6 * n - 2)
                        settle(pool)
                        pool.indirect_dma_start(out=xe[0][0:SLOTS, :], out_offset=None, in_=xg, in_offset=rows_of(0)) \
                            .then_inc(S['ov_gath'], 16)
                        pool.wait_ge(S['ov_ye'], 2 * n)
                        settle(pool)
                        pool.indirect_dma_start(out=yd, out_offset=rows_of(0), in_=ye[0][0:SLOTS, :],
                                                in_offset=None, compute_op=ALU.add).then_inc(S['ov_scat'], 16)
                        pool.wait_ge(S['ov_scat'], 16 * n)
            gp.memset(zrow[:, 0:1], 0.0).then_inc(S['moe_done'], 1)

        @block.sync
        def _(sp):
            sp.dma_start(const, A['const']).then_inc(S['consts_in'], 16)
            sp.dma_start(xrow[:, 0:2, :], A['x_prompt'][0].rearrange("(t p) d -> p t d", p=128)) \
              .then_inc(S['x_in'], 16)
            sp.dma_start(xrow[0:NS, 2, :], A['x_sample'][:, 0, :]).then_inc(S['small_in'], 16)
            sp.dma_start(shiftrows[0:NS, :], A['state_shift'][0]).then_inc(S['small_in'], 16)
            sp.dma_start(grow, A['norm1_g'][0:1, :].partition_broadcast(128)).then_inc(S['small_in'], 16)
            n = 0
            for v in VECS:
                r = VROWS.get(v, KT)
                src = A[v].rearrange("a h n -> a (h n)") if v == 'r_k' else A[v]
                sp.dma_start(vecrows[n:n + r, :], src[0].rearrange("(r c) -> r c", c=128)) \
                  .then_inc(S['vec_in'], 16)
                n += r
            sp.dma_start(convrows[0:CW, :], A['conv_w'][0]).then_inc(S['vec_in'], 16)
            for q in range(1 + NSEC * NG):
                c0 = C_LORA if q == 0 else GROUP_SECTIONS[(q - 1) % NSEC] + 256 * ((q - 1) // NSEC)
                if q >= NW:
                    sp.wait_ge(S['zt_mm'], 2 * (q - NW) + 2)
                sp.dma_start(wring[q % NW], w_in[:, :, c0:c0 + 256]).then_inc(win_in[q % NW], 16)
                if q == 1:
                    sp.dma_start(wlora[0:64, :], A['w_decay_up'][0]).then_inc(S['lora_in'], 16)
                    sp.dma_start(wlora[64:128, :], A['a_up'][0]).then_inc(S['lora_in'], 16)
                    sp.dma_start(wgate, A['g_up'][0]).then_inc(S['lora_in'], 16)
            sp.wait_ge(S['ma_ready'], NG)
            sp.wait_ge(S['c_ready'], NG)
            sp.wait_ge(S['state_out'], 16 * 2 * NG)
            sp.wait_ge(S['conv_out'], 16 * 2 * NG)
            sp.wait_ge(S['samp_out'], 16 * NS * NG)
            for h in range(2):
                sp.dma_start(w_out_sb[:, :, 512 * h:512 * h + 512],
                             A['w_out'][0].rearrange("(k p) c -> p k c", p=128)[:, :, 512 * h:512 * h + 512]) \
                  .then_inc(S['wout_in'], 16)
            sp.dma_start(hrow_x[:, 0:2, :], A['x_prompt'][0].rearrange("(t p) d -> p t d", p=128)) \
              .then_inc(S['hx_in'], 16)
            sp.dma_start(hrow_x[0:NS, 2, :], A['x_sample'][:, 0, :]).then_inc(S['hx_in'], 16)
            moe_sp(sp)

        @block.tensor
        def _(pe):
            note, link = counted(pe)

            def mm(out_, lhsT, rhs, start=True, stop=True):
                return nc.tensor.matmul(out_, lhsT=lhsT, rhs=rhs, start=start, stop=stop)

            pe.wait_ge(S['consts_in'], 16)
            for t in range(2):
                pe.wait_ge(S['xn_ready'], t + 1)
                for k in range(KT):
                    ins = nc.tensor.transpose(B[2 * t + k // 4][:, 128 * (k % 4):128 * (k % 4) + 128],
                                              xrow[:, t, 128 * k:128 * k + 128], ident)
                    if k % 4 == 3:
                        note(ins, 'xt_mm')
            pe.wait_ge(S['xn_ready'], 3)
            pe.wait_ge(S['small_in'], 48)
            for k in range(KT):
                nc.tensor.transpose(B[4][:, 16 * k:16 * k + 8], xrow[0:NS, 2, 128 * k:128 * k + 128],
                                    ident[0:NS, 0:NS])
                ins = nc.tensor.transpose(B[4][:, 16 * k + 8:16 * k + 16], shiftrows[0:NS, 128 * k:128 * k + 128],
                                          ident[0:NS, 0:NS])
            note(ins, 'xt_mm')
            pe.wait_ge(S['vec_in'], 16 * (len(VECS) + 1))
            nc.tensor.transpose(B[5][:, 0:NVEC], vecrows[0:NVEC, :], ident[0:NVEC, 0:NVEC])
            for k in range(KT):
                ins = nc.tensor.transpose(B[5][:, 128 + CW * k:128 + CW * k + CW],
                                          convrows[0:CW, 128 * k:128 * k + 128], ident[0:CW, 0:CW])
            note(ins, 'vec_mm')

            def z_tile(n):
                q = n // 2
                if n % 2 == 0:
                    pe.wait_ge(win_in[q % NW], 16 * (q // NW + 1))
                z_wait_free(pe, n)
                for k in range(KT):
                    ins = mm(ZP[n % 2][:, 0:NCOL], wring[q % NW][:, k, 128 * (n % 2):128 * (n % 2) + 128],
                             xT[:, k, :], k == 0, k == KT - 1)
                note(ins, 'zt_mm')

            pe.wait_ge(S['xt_ready'], 6)
            z_tile(0)
            z_tile(1)
            pe.wait_ge(S['lora_in'], 48)
            pe.wait_ge(S['lora_ready'], 3)
            ring = [0]

            for g in range(NG):
                z0 = 2 + NZ * g

                def ring_bank():
                    i = ring[0]
                    ring[0] += 1
                    wait(pe, 'tr_free', i - 2)
                    return B[(1, 4, 5)[i % 3]]

                wait(pe, 'ma_ready', g)
                if g == 0:
                    pe.wait_ge(S['vec_ready'], 2)
                for p in range(2):
                    c = slice(256 * g + 128 * p, 256 * g + 128 * p + 128)
                    note(mm(B[p][:, 0:NCOL], wlora[0:64, c], TW[0:64, :]), 'lora_mm')
                for p in range(2):
                    c = slice(256 * g + 128 * p, 256 * g + 128 * p + 128)
                    note(mm(B[2 + p][:, 0:NCOL], wlora[64:128, c], TW[64:128, :]), 'lora_mm')
                for p in range(2):
                    c = slice(256 * g + 128 * p, 256 * g + 128 * p + 128)
                    note(mm(B[4 + p][:, 0:NCOL], wgate[:, c], SG), 'lora_mm')
                for i in range(8):
                    z_tile(z0 + i)
                pe.wait_ge(S['sq_ready'], g + 1)
                pe.wait_ge(S['lora_free'], 6 * (g + 1))
                for p in range(2):
                    note(mm(B[p][:, 0:NCOL], K['same_head'], SQ[:, p, :]), 'ss_mm')
                z_tile(z0 + 8)
                z_tile(z0 + 9)
                pe.wait_ge(S['plain_ready'], 4 * (g + 1))
                pe.wait_ge(S['pbd_ready'], 6 * (g + 1))
                pe.wait_ge(S['root_ready'], 2 * (g + 1))
                arf = AR.rearrange("p u w n -> p u (w n)")
                for h in range(2):
                    for u in range(4 * h, 4 * h + 4):
                        ins = mm(B[2 + h][:, 128 * (u % 4):128 * (u % 4) + 128], b_bd[:, u, :], arf[:, u, :])
                    note(ins, 'a_mm')
                for u in range(NU):
                    ins = mm(B[0][:, CH * u:CH * u + CH], a_bd[:, u, :], BP[:, u, :])
                note(ins, 'a_mm')
                for h in range(2):
                    for u in range(4 * h, 4 * h + 4):
                        ins = mm(B[4 + h][:, 128 * (u % 4):128 * (u % 4) + 128], k_bd[:, u, :], arf[:, u, :])
                    note(ins, 'a_mm')
                z_tile(z0 + 10)
                pe.wait_ge(S['lmask_ready'], 4 * (g + 1))

                def tr_units(src, h):
                    bank = ring_bank()
                    for u in range(4 * h, 4 * h + 4):
                        ins = nc.tensor.transpose(bank[:, 128 * (u % 4):128 * (u % 4) + 128], src[:, u, :], ident)
                    note(ins, 'tr_mm')

                def tr_v(p):
                    bank = ring_bank()
                    for c in range(NCH):
                        ins = nc.tensor.transpose(
                            bank[:, 128 * c:128 * c + 128],
                            VD[:, NCH * p + c, :, :].rearrange("p r n -> p (r n)"), ident)
                    note(ins, 'tr_mm')

                def tr_samples():
                    bank = ring_bank()
                    for p in range(2):
                        ins = nc.tensor.transpose(bank[0:48, 128 * p:128 * p + 128],
                                                  QS[:, p, :, :].rearrange("p q s -> p (q s)"), ident)
                    note(ins, 'tr_mm')

                def tr_conv_state():
                    pe.wait_ge(scr_in, 16 * (g + 1))
                    bank = ring_bank()
                    for p in range(2):
                        for h in range(2):
                            ins = nc.tensor.transpose(bank[:, 240 * p + 120 * h:240 * p + 120 * h + 120],
                                                      SCR[0:120, h, 128 * p:128 * p + 128], ident[0:120, 0:120])
                    note(ins, 'tr_mm')

                def tr_new_conv():
                    bank = ring_bank()
                    for p in range(2):
                        ins = nc.tensor.transpose(bank[0:46, 128 * p:128 * p + 128], UU[:, p, 256:302], ident)
                    note(ins, 'tr_mm')

                between = [
                    lambda: (tr_units(b_bd, 0), tr_units(b_bd, 1), tr_samples(), tr_conv_state(), z_tile(z0 + 11)),
                    lambda: (tr_units(k_bd, 0), tr_units(k_bd, 1), z_tile(z0 + 12)),
                    lambda: (tr_v(0), tr_v(1), z_tile(z0 + 13)),
                    lambda: tr_new_conv(),
                    lambda: None,
                ]
                pe.wait_ge(S['lbd_ready'], 4 * (g + 1))
                pe.wait_ge(S['qs_ready'], 6 * (g + 1))
                pe.wait_ge(S['vd_ready'], g + 1)
                for i, m in enumerate(LEVELS):
                    last = i == len(LEVELS) - 1
                    pe.wait_ge(S['t_ready'], 5 * g + i + 1)
                    for u in range(NU):
                        ins = mm(B[0][:, CH * u:CH * u + CH], LT_bd[:, u, :], T_st[:, u, :])
                    note(ins, 'y_mm')
                    between[i]()
                    pe.wait_ge(S['y_ready'], 5 * g + i + 1)
                    pe.wait_ge(S['tt_ready'], 6 * g + i + 1)
                    if not last:
                        pe.wait_ge(S['ttbd_act'], 6 * g + i + 1)
                        pe.wait_ge(S['ttbd_pool'], 6 * g + i + 1)
                        for u in range(NU):
                            ins = mm(B[2][:, CH * u:CH * u + CH], TT_bd[:, u, :], Y_st[:, u, :])
                        note(ins, 't_mm')
                    pe.wait_ge(S['ybd_act'], 5 * g + i + 1)
                    pe.wait_ge(S['ybd_pool'], 5 * g + i + 1)
                    for u in range(NU):
                        ins = mm(B[3][:, CH * u:CH * u + CH], Y_bd[:, u, :], TT_st[:, u, :])
                    note(ins, 'tt_mm')
                pe.wait_ge(S['ttbd_act'], 6 * g + 6)
                pe.wait_ge(S['ttbd_pool'], 6 * g + 6)
                pe.wait_ge(S['tr_free'], 11 * g + 9)
                pe.wait_ge(S['state_zero'], 2 * (g + 1))
                for c in range(NCH):
                    n = NCH * g + c
                    if c:
                        pe.wait_ge(S['s_ready'], n)
                    for p in range(2):
                        u = NCH * p + c
                        mm(B[0][:, CH * p:CH * p + CH], a_bd[:, u, :], S_st[:, p, :], True, False)
                        ins = mm(B[0][:, CH * p:CH * p + CH], AK_bd[:, u, :], V_st[:, u, :], False, True)
                    note(ins, 'zq_mm')
                    pe.wait_ge(S['zq_ready'], n + 1)
                    for p in range(2):
                        ins = mm(B[2][:, CH * p:CH * p + CH], TT_bd[:, NCH * p + c, :], Z_st[:, p, :])
                    note(ins, 'u_mm')
                    pe.wait_ge(S['ust_ready'], n + 1)
                    for p in range(2):
                        u = NCH * p + c
                        mm(B[0][:, 128 + CH * p:128 + CH * p + CH], BT_bd[:, u, :], U_st[:, p, :], True, False)
                        ins = mm(B[0][:, 128 + CH * p:128 + CH * p + CH], KTok_bd[:, u, :], V_st[:, u, :], False, True)
                    note(ins, 's_mm')
                    pe.wait_ge(S['ubd_ready'], 2 * (n + 1))
                    if c:
                        pe.wait_ge(S['sbd_ready'], 2 * n)
                        pe.wait_ge(S['o_ready'], n)
                    for p in range(2):
                        u = NCH * p + c
                        o = B[3][:, CH * p:CH * p + CH]
                        mm(o, S_bd[:, p, :], AR[:, u, 1, :], True, False)
                        mm(o, U_bd[:, p, :], X1[:, u, 1, :], False, False)
                        ins = mm(o, V_bd[:, u, :], X2[:, u, 1, :], False, True)
                    note(ins, 'o_mm')
                bank = ring_bank()
                pe.wait_ge(S['sbd_ready'], 2 * NCH * (g + 1))
                for p in range(2):
                    ins = nc.tensor.transpose(bank[:, 128 * p:128 * p + 128], S_bd[:, p, :], ident)
                note(ins, 'tr_mm')
                bank = ring_bank()
                pe.wait_ge(S['os_in'], 16 * (g + 1))
                for p in range(2):
                    ins = nc.tensor.transpose(bank[:, NS * p:NS * p + NS], OR[0:NS, 128 * p:128 * p + 128],
                                              ident[0:NS, 0:NS])
                note(ins, 'tr_mm')
                pe.wait_ge(S['o_ready'], NCH * (g + 1))
                pe.wait_ge(S['tr_free'], 11 * (g + 1))
                for p in range(2):
                    note(mm(B[p][:, 0:NCOL], K['same_head'], O[:, p, :]), 'gm_mm')
                pe.wait_ge(S['bo_in'], g + 1)
                for p in range(2):
                    note(mm(B[4 + p][:, 0:NCOL], K['same_head'], KK[:, p, :]), 'bo_mm')
                pe.wait_ge(S['gsq_ready'], g + 1)
                for p in range(2):
                    note(mm(B[2 + p][:, 0:NCOL], K['same_head'], SQ[:, p, :]), 'gv_mm')

            pe.wait_ge(S['ma_ready'], NG)
            pe.wait_ge(S['c_ready'], NG)
            for k in range(KT):
                ins = mm(ZP[0][:, 0:NCOL], K['ones'], C[:, k, :], k == 0, k == KT - 1)
            note(ins, 'cm_mm')
            pe.wait_ge(S['csq_ready'], 1)
            for k in range(KT):
                ins = mm(ZP[1][:, 0:NCOL], K['ones'], CS[:, k, :], k == 0, k == KT - 1)
            note(ins, 'cv_mm')
            pe.wait_ge(S['wout_in'], 32)
            for k in range(KT):
                pe.wait_ge(S['merged_ready'], k + 1)
                for t in range(3):
                    lhsT = MA[:, k, 128 * t:128 * t + 128] if t < 2 else MA[:, k, NP + 1:NCOL:2]
                    rows = 128 if t < 2 else NS
                    for h in range(2):
                        ins = mm(B[2 * t + h][0:rows, :], lhsT, w_out_sb[:, k, 512 * h:512 * h + 512],
                                 k == 0, k == KT - 1)
            note(ins, 'wo_mm')
            moe_pe(pe, note, mm)

        @block.scalar
        def _(act):
            note, link = counted(act)

            def fn(out_, in_, f, **kw):
                return nc.scalar.activation(out_, in_, f, **kw)

            act.wait_ge(S['consts_in'], 16)
            act.wait_ge(S['x_in'], 16)
            for t in range(3):
                rows = 128 if t < 2 else NS
                if t == 2:
                    act.wait_ge(S['small_in'], 48)
                link(fn(junk[0:rows, :], xrow[0:rows, t, :], ACT.Square, accum_out=stat[0:rows, t:t + 1]), 'act_chain')
                note(fn(stat[0:rows, 3 + t:4 + t], stat[0:rows, t:t + 1], ACT.Sqrt,
                        scale=1.0 / D, bias=K['rms_eps'][0:rows, :]), 'xstd_ready')
            for i in range(4):
                act.wait_ge(S['xt_mm'], i + 1)
                t, h = i // 2, i % 2
                note(fn(xT[:, 4 * h:4 * h + 4, 128 * t:128 * t + 128],
                        B[i][:, :].rearrange("p (k c) -> p k c", k=4), ACT.Copy), 'xt_ready')
            act.wait_ge(S['xt_mm'], 5)
            b4 = B[4][:, 0:128].rearrange("p (k w s) -> p w k s", k=KT, w=2)
            note(fn(xT[:, :, NP + 1:NCOL:2], b4[:, 0], ACT.Copy), 'xt_ready')
            note(fn(xT[:, :, NP:NCOL:2], b4[:, 1], ACT.Copy), 'xt_ready')
            act.wait_ge(S['vec_mm'], 1)
            note(fn(VC, B[5][:, 0:NVEC], ACT.Copy), 'vec_ready')
            note(fn(CWT.rearrange("p k w -> p (k w)"), B[5][:, 128:128 + KT * CW], ACT.Copy), 'vec_ready')
            act.wait_ge(S['vec_ready'], 1)
            act.wait_ge(S['zero_ready'], 1)
            act.wait_ge(S['bd_zero'], 1)

            def shift_part(n, i):
                act.wait_ge(S['zt_mm'], n + 1)
                note(fn(zs[:, n % 2, 1:NCOL + 1], ZP[n % 2][:, 0:NCOL], ACT.Copy, scale=mucol(i)), 'zs_ready')

            shift_part(0, 24)
            shift_part(1, 25)
            act.wait_ge(S['z_free_dve'], 1)
            note(fn(TW[0:64, :], LZ[0:64, 0, 0, :], ACT.Tanh), 'lora_ready')
            note(fn(TW[64:128, :], LZ[64:128, 0, 0, :], ACT.Copy), 'lora_ready')
            act.wait_ge(S['z_free_dve'], 2)
            note(fn(SG, LZ[:, 0, 1, :], ACT.Sigmoid), 'lora_ready')
            ring = [0]

            for g in range(NG):
                z0 = 2 + NZ * g

                def from_ring():
                    i = ring[0]
                    ring[0] += 1
                    act.wait_ge(S['tr_mm'], i + 1)
                    return B[(1, 4, 5)[i % 3]]

                for p in range(2):
                    act.wait_ge(S['lora_mm'], 6 * g + p + 1)
                    note(fn(DC[:, p, :], B[p][:, 0:NCOL], ACT.Sigmoid, bias=vcol('w0', 2 * g + p)), 'lora_free')
                for p in range(2):
                    act.wait_ge(S['lora_mm'], 6 * g + p + 3)
                    note(fn(AA[:, p, :], B[2 + p][:, 0:NCOL], ACT.Sigmoid, bias=vcol('a0', 2 * g + p)), 'lora_free')
                for p in range(2):
                    act.wait_ge(S['lora_mm'], 6 * g + p + 5)
                    note(fn(G[:, p, :], B[4 + p][:, 0:NCOL], ACT.Copy), 'lora_free')
                act.wait_ge(S['lora_free'], 6 * g + 2)
                note(fn(DC, DC, ACT.Exp, scale=-EXP_M05), 'dec_ready')
                for i in range(6):
                    sec, p = i // 2, i % 2
                    shift_part(z0 + i, 8 * sec + 2 * g + p)
                for p in range(2):
                    act.wait_ge(S['zt_mm'], z0 + 6 + p + 1)
                    note(fn(SB[:, p, :], ZP[(z0 + 6 + p) % 2][:, 0:NCOL], ACT.Sigmoid), 'z_free_act')
                for p in range(2):
                    act.wait_ge(S['ss_mm'], 2 * g + p + 1)
                    note(fn(INV[:, p, :], B[p][:, 0:NCOL], ACT.Sqrt), 'root_ready')

                def gate_tile(i):
                    act.wait_ge(S['zt_mm'], z0 + i + 1)
                    dst = GA[:, i - 10, :] if i < 12 else GB[:, 2 * g + i - 12, :]
                    note(fn(dst, ZP[(z0 + i) % 2][:, 0:NCOL], ACT.Sigmoid), 'z_free_act')

                def copy_units(dst, h):
                    b = from_ring()
                    note(fn(dst[:, 4 * h:4 * h + 4, :].rearrange("p u n -> p (u n)"), b[:, :], ACT.Copy), 'tr_free')

                def copy_v(p):
                    b = from_ring()
                    bu = b[:, :].rearrange("p (u n) -> p u n", u=NCH)
                    for lo, hi in halves:
                        nc.scalar.activation(V_bd[lo:hi, NCH * p:NCH * p + NCH, lo:hi], bu[lo:hi, :, lo:hi], ACT.Copy)
                    fn(V_st[0:64, NCH * p:NCH * p + NCH, :], bu[0:64, :, 0:64], ACT.Copy)
                    note(fn(V_st[64:128, NCH * p:NCH * p + NCH, :], bu[64:128, :, 64:128], ACT.Copy), 'tr_free')

                def copy_samples():
                    b = from_ring()
                    wait(act, 'qv_sent', 16 * g)
                    note(fn(QR[0:48, :], b[0:48, 0:256], ACT.Copy), 'tr_free')

                def copy_conv_state():
                    b = from_ring()
                    for p in range(2):
                        ins = fn(SCB[:, p, :, 0:CW - 1],
                                 b[:, 240 * p:240 * p + 240].rearrange("p (s w) -> p s w", s=NS), ACT.Copy)
                    note(ins, 'tr_free')

                def copy_new_conv():
                    b = from_ring()
                    wait(act, 'conv_out', 32 * g)
                    note(fn(UR[0:46, :], b[0:46, 0:256], ACT.Copy), 'tr_free')

                gate_tile(10)
                evacuate = [
                    lambda: (copy_units(BT_bd, 0), copy_units(BT_bd, 1), copy_samples(), copy_conv_state()),
                    lambda: (copy_units(KTok_bd, 0), copy_units(KTok_bd, 1)),
                    lambda: (copy_v(0), copy_v(1)),
                    lambda: copy_new_conv(),
                    lambda: None,
                ]
                act.wait_ge(S['tt_ready'], 6 * g + 1)
                note(fn(TT_bd[0:64, :, 0:64], TT_st[0:64, :, :], ACT.Copy), 'ttbd_act')
                for i, m in enumerate(LEVELS):
                    evacuate[i]()
                    act.wait_ge(S['y_ready'], 5 * g + i + 1)
                    note(fn(Y_bd[0:64, :, 0:64], Y_st[0:64, :, :], ACT.Copy), 'ybd_act')
                    if i < 3:
                        gate_tile(11 + i)
                    act.wait_ge(S['tt_ready'], 6 * g + i + 2)
                    note(fn(TT_bd[0:64, :, 0:64], TT_st[0:64, :, :], ACT.Copy), 'ttbd_act')
                for c in range(NCH):
                    n = NCH * g + c
                    act.wait_ge(S['zq_mm'], n + 1)
                    note(fn(Z_st.rearrange("p a n -> p (a n)"), B[0][:, 0:128], ACT.Copy), 'zq_ready')
                    act.wait_ge(S['u_mm'], n + 1)
                    note(fn(U_st.rearrange("p a n -> p (a n)"), B[2][:, 0:128], ACT.Copy), 'ust_ready')
                b = from_ring()
                wait(act, 'state_out', 32 * g)
                note(fn(SO.rearrange("p a n -> p (a n)"), b[:, 0:256], ACT.Copy), 'tr_free')
                b = from_ring()
                act.wait_ge(S['o_ready'], NCH * (g + 1))
                note(fn(O[:, :, NP + 1:NCOL:2], b[:, 0:2 * NS].rearrange("p (a s) -> p a s", a=2), ACT.Copy), 'tr_free')
                act.wait_ge(S['gd_ready'], g + 1)
                note(fn(SQ, O, ACT.Square), 'gsq_ready')
                for p in range(2):
                    act.wait_ge(S['gv_mm'], 2 * g + p + 1)
                    note(fn(INV[:, p, :], B[2 + p][:, 0:NCOL], ACT.Sqrt, scale=1.0 / CH, bias=K['gn_eps']), 'gstd_ready')

            act.wait_ge(S['cd_ready'], 1)
            note(fn(CS, CD, ACT.Square), 'csq_ready')
            act.wait_ge(S['cv_mm'], 1)
            note(fn(lnr, ZP[1][:, 0:NCOL], ACT.Sqrt, scale=1.0 / D, bias=K['ln_eps']), 'cstd_ready')
            for k in range(KT):
                act.wait_ge(S['cn_ready'], k + 1)
                note(fn(CS[:, k, :], CD[:, k, :], ACT.Sigmoid), 'cs_sig')
            moe_act(act, note, link, fn)

        @block.vector
        def _(dve):
            note, link = counted(dve)
            v = nc.vector
            M, AD, SU = ALU.mult, ALU.add, ALU.subtract
            chain = 'dve_chain'

            v.memset(zs[:, :, 0:1], 0.0)
            v.memset(C, 0.0)
            v.memset(UU[:, :, 0:CW - 1], 0.0)
            note(v.memset(PP[:, :, :, 0:1], 1.0), 'zero_ready')

            dve.wait_ge(S['small_in'], 48)
            for t in range(3):
                rows = 128 if t < 2 else NS
                dve.wait_ge(S['xstd_ready'], t + 1)
                link(v.reciprocal(stat[0:rows, 6 + t:7 + t], stat[0:rows, 3 + t:4 + t]), chain)
                link(v.scalar_tensor_tensor(out=xrow[0:rows, t, :], in0=xrow[0:rows, t, :],
                                            scalar=stat[0:rows, 6 + t:7 + t], in1=grow[0:rows, :],
                                            op0=M, op1=M), 'xn_ready')
            dve.wait_ge(S['vec_ready'], 2)
            mu0, ka0 = VOFF['mu_shift'], VOFF['k_a']
            v.tensor_scalar(omu, VC[:, mu0:mu0 + 26], -1.0, 1.0, M, AD)
            link(v.tensor_scalar(oka, VC[:, ka0:ka0 + KT], -1.0, 1.0, M, AD), chain)

            def shifted(n, i, dst):
                dve.wait_ge(S['zs_ready'], (n if n < 2 else 2 + 6 * ((n - 2) // NZ) + (n - 2) % NZ) + 1)
                note(v.scalar_tensor_tensor(out=dst, in0=ZP[n % 2][:, 0:NCOL], scalar=omu[:, i:i + 1],
                                            in1=zs[:, n % 2, 0:NCOL], op0=M, op1=AD), 'z_free_dve')

            shifted(0, 24, LZ[:, 0, 0, :])
            shifted(1, 25, LZ[:, 0, 1, :])
            dve.wait_ge(S['lora_ready'], 3)

            for g in range(NG):
                z0 = 2 + NZ * g
                zf = 2 + 8 * g
                col = lambda name, p: vcol(name, 2 * g + p)
                tok = lambda x: x[:, :, 0:NP].rearrange("p a (c n) -> p a c n", n=CH)
                unit = lambda x: x.rearrange("p (a c) n -> p a c n", a=2)
                for i in range(6):
                    shifted(z0 + i, 8 * (i // 2) + 2 * g + i % 2, LZ[:, i // 2, i % 2, :])
                dve.wait_ge(S['z_free_dve'], zf + 6)
                R_, K_, V_ = LZ[:, 0], LZ[:, 1], LZ[:, 2]
                for p in range(2):
                    link(v.tensor_scalar(KK[:, p, :], K_[:, p, :], col('k_k', p), None, M), chain)
                link(v.tensor_tensor(SQ, KK, KK, M), 'sq_ready')
                note(v.tensor_copy(VD.rearrange("p (a c) r n -> p a c r n", a=2)[:, 0],
                                   tok(V_)[:, 0].unsqueeze(2).broadcast_to([128, NCH, 2, CH])), chain)
                note(v.tensor_copy(VD.rearrange("p (a c) r n -> p a c r n", a=2)[:, 1],
                                   tok(V_)[:, 1].unsqueeze(2).broadcast_to([128, NCH, 2, CH])), 'vd_ready')
                dve.wait_ge(S['dec_ready'], g + 1)
                for p in range(2):
                    for c in range(NCH):
                        ins = v.tensor_tensor_scan(PP[:, p, c, 1:CH + 1], DC[:, p, CH * c:CH * c + CH],
                                                   K['ones'][:, 0:CH], 1.0, M, M)
                        note(ins, chain)
                for p in range(2):
                    link(v.tensor_scalar(INV2[:, p, :], AA[:, p, :], col('k_a', p), oka[:, 2 * g + p:2 * g + p + 1],
                                         M, AD), chain)
                link(v.reciprocal(IP, PP[:, :, :, 1:CH + 1]), chain)
                link(v.tensor_tensor(K_, K_, INV2, M), chain)
                dve.wait_ge(S['root_ready'], 2 * (g + 1))
                link(v.tensor_scalar(INV, INV, 1e-12, None, ALU.max), chain)
                link(v.reciprocal(INV, INV), chain)
                link(v.tensor_tensor(KK, KK, INV, M), chain)
                link(v.tensor_tensor(AA, KK, AA, M), chain)
                prev, cur = PP[:, :, :, 0:CH], PP[:, :, :, 1:CH + 1]
                for p in range(2):
                    u4 = slice(NCH * p, NCH * p + NCH)
                    ins = v.scalar_tensor_tensor(out=AR[:, u4, 0, :], in0=tok(KK)[:, p], scalar=-1.0,
                                                 in1=prev[:, p], op0=M, op1=M)
                note(ins, 'plain_ready')
                note(v.tensor_tensor(unit(BP), tok(AA), IP, M), 'plain_ready')
                note(v.tensor_tensor(unit(KP), tok(K_), IP, M), 'plain_ready')
                for p in range(2):
                    u4 = slice(NCH * p, NCH * p + NCH)
                    ins = v.tensor_tensor(AR[:, u4, 1, :], tok(R_)[:, p], cur[:, p], M)
                link(ins, 'plain_ready')
                for p in range(2):
                    n = z0 + 8 + p
                    dve.wait_ge(S['z_free_act'], 6 * g + p + 1)
                    dve.wait_ge(S['zt_mm'], n + 1)
                    if p == 0:
                        wait(dve, 'tr_free', 11 * g)
                    link(v.tensor_tensor(UU[:, p, CW - 1:CW - 1 + NCOL], ZP[n % 2][:, 0:NCOL], SB[:, p, :], M),
                         'z_free_dve')
                link(v.tensor_copy(SCB[:, :, :, CW - 1], UU[:, :, CW - 1 + NP + 1:CW - 1 + NCOL:2]), chain)
                up = K['upper'].rearrange("p (w n) -> p w n", w=2)
                for h in range(2):
                    dve.wait_ge(S['a_mm'], 5 * g + h + 1)
                    note(v.tensor_tensor(X1[:, 4 * h:4 * h + 4],
                                         B[2 + h][:, :].rearrange("p (u w n) -> p u w n", u=4, w=2),
                                         up.unsqueeze(1).broadcast_to([128, 4, 2, CH]), M), 'lmask_ready')
                dve.wait_ge(S['lmask_ready'], 4 * g + 2)
                bc = lambda k: K[k].unsqueeze(1).broadcast_to([128, NU, CH])
                bank = lambda i: B[i][:, :].rearrange("p (u n) -> p u n", u=NU)
                dve.wait_ge(S['a_mm'], 5 * g + 3)
                link(v.tensor_tensor(T_st, bank(0), bc('pair_low'), M), chain)
                link(v.tensor_tensor(T_st, T_st, bc('eye_st'), AD), 't_ready')
                link(v.tensor_tensor(TT_st, X1[:, :, 0, :], bc('pair_up'), M), chain)
                link(v.tensor_tensor(TT_st, TT_st, bc('eye_st'), AD), 'tt_ready')
                for h in range(2):
                    dve.wait_ge(S['a_mm'], 5 * g + h + 4)
                    note(v.tensor_tensor(X2[:, 4 * h:4 * h + 4],
                                         B[4 + h][:, :].rearrange("p (u w n) -> p u w n", u=4, w=2),
                                         up.unsqueeze(1).broadcast_to([128, 4, 2, CH]), M), 'lmask_ready')

                def taps():
                    for w in range(CW):
                        for p in range(2):
                            acc, u = C[:, 2 * g + p, 0:NP], UU[:, p, w:w + NP]
                            cw = CWT[:, 2 * g + p, w:w + 1]
                            if w:
                                dve.wait_ge(S['tap'], 62 * g + 2 * w + p - 1)
                            if w == 0:
                                note(v.tensor_scalar(acc, u, cw, col('conv_b', p), M, AD), 'tap')
                            else:
                                note(v.scalar_tensor_tensor(out=acc, in0=u, scalar=cw, in1=acc, op0=M, op1=AD), 'tap')
                            yield

                tap = taps()

                def some_taps(n):
                    for _ in range(n):
                        next(tap, None)

                for i, m in enumerate(LEVELS):
                    some_taps(2)
                    dve.wait_ge(S['y_mm'], 5 * g + i + 1)
                    wait(dve, 'tt_mm', 5 * g + i)
                    link(v.tensor_tensor(Y_st, bank(0), bc(f'level{m}'), M), 'y_ready')
                    some_taps(4)
                    if i < len(LEVELS) - 1:
                        dve.wait_ge(S['t_mm'], 4 * g + i + 1)
                        link(v.tensor_tensor(T_st, T_st, bank(2), AD), 't_ready')
                    dve.wait_ge(S['tt_mm'], 5 * g + i + 1)
                    dve.wait_ge(S['ttbd_act'], 6 * g + i + 1)
                    dve.wait_ge(S['ttbd_pool'], 6 * g + i + 1)
                    link(v.tensor_tensor(TT_st, TT_st, bank(3), AD), 'tt_ready')

                qk = lambda q: QV[:, q, :].unsqueeze(1).broadcast_to([128, 16, CH])
                row = lambda x: x.unsqueeze(2).broadcast_to([128, 16, CH])

                def sample_part(c):
                    if c == 0:
                        dve.wait_ge(S['qv_in'], 16 * 5 * (g + 1))
                        dve.wait_ge(S['sst_in'], 16 * 8 * (g + 1))
                        link(v.tensor_tensor(SMT, SM, qk(4), M), chain)
                        link(v.tensor_reduce(SA, SMT, AX.X, AD), chain)
                        link(v.tensor_tensor(SM, SM, qk(1), M), chain)
                    elif c == 1:
                        link(v.tensor_tensor(SMT, row(SA), qk(5), M), chain)
                        link(v.tensor_tensor(SM, SM, SMT, SU), chain)
                    elif c == 2:
                        link(v.tensor_tensor(SMT, row(QVV), qk(2), M), chain)
                        link(v.tensor_tensor(SM, SM, SMT, AD), 'sm_ready')
                    else:
                        link(v.tensor_tensor(SMT, SM, qk(0), M), chain)
                        link(v.tensor_reduce(OS, SMT, AX.X, AD), 'os_ready')

                wait(dve, 's_mm', NCH * g)
                wait(dve, 'o_mm', NCH * g)
                wait(dve, 'sbd_ready', 2 * NCH * g)
                if g == 0:
                    dve.wait_ge(S['bd_zero'], 1)
                wait(dve, 'tr_free', 11 * g)
                v.memset(S_st, 0.0)
                note(v.memset(S_bd[0:64, :, 0:64], 0.0), 'state_zero')
                note(v.memset(S_bd[64:128, :, 64:128], 0.0), 'state_zero')
                dve.wait_ge(S['state_zero'], 2 * (g + 1))
                for c in range(NCH):
                    n = NCH * g + c
                    some_taps(3)
                    sample_part(c)
                    dve.wait_ge(S['s_mm'], n + 1)
                    if c:
                        dve.wait_ge(S['sbd_ready'], 2 * n)
                    link(v.tensor_tensor(S_st, S_st, B[0][:, 128:256].rearrange("p (a n) -> p a n", a=2), AD), chain)
                    for p in range(2):
                        ins = v.tensor_scalar(S_st[:, p, :], S_st[:, p, :], PP[:, p, c, CH:CH + 1], None, M)
                        if p == 0:
                            note(ins, chain)
                    link(ins, 's_ready')
                    dve.wait_ge(S['o_mm'], n + 1)
                    link(v.tensor_copy(O[:, :, CH * c:CH * c + CH], B[3][:, 0:128].rearrange("p (a n) -> p a n", a=2)),
                         'o_ready')
                link(v.tensor_tensor(KK, R_, K_, M), chain)
                for p in range(2):
                    ins = v.tensor_scalar(KK[:, p, :], KK[:, p, :], col('r_k', p), None, M)
                    if p == 0:
                        link(ins, chain)
                link(ins, 'bo_in')
                for p in range(2):
                    dve.wait_ge(S['gm_mm'], 2 * g + p + 1)
                    ins = v.scalar_tensor_tensor(out=O[:, p, :], in0=B[p][:, 0:NCOL], scalar=-1.0 / CH,
                                                 in1=O[:, p, :], op0=M, op1=AD)
                    if p == 0:
                        link(ins, chain)
                link(ins, 'gd_ready')
                some_taps(62)
                for p in range(2):
                    link(v.tensor_tensor(SCT, SCB[:, p], CWT[:, 2 * g + p].unsqueeze(1).broadcast_to([128, NS, CW]), M),
                         chain)
                    link(v.tensor_reduce(SCR8, SCT, AX.X, AD), chain)
                    link(v.tensor_scalar(C[:, 2 * g + p, NP + 1:NCOL:2], SCR8, col('conv_b', p), None, AD), chain)
                dve.wait_ge(S['tap'], 62 * (g + 1))
                note(v.memset(zero1, 0.0), 'c_ready')
                dve.wait_ge(S['gstd_ready'], 2 * (g + 1))
                link(v.reciprocal(INV, INV), chain)
                link(v.tensor_tensor(O, O, INV, M), chain)
                for p in range(2):
                    link(v.tensor_scalar(O[:, p, :], O[:, p, :], col('gn_g', p), col('gn_b', p), M, AD), chain)
                for p in range(2):
                    dve.wait_ge(S['bo_mm'], 2 * g + p + 1)
                    link(v.tensor_tensor(INV[:, p, :], B[4 + p][:, 0:NCOL], V_[:, p, :], M), chain)
                link(v.tensor_tensor(O, O, INV, AD), chain)
                link(v.tensor_tensor(O, O, G, M), chain)
                dve.wait_ge(S['z_free_act'], 6 * g + 6)
                link(v.tensor_tensor(MA[:, 2 * g:2 * g + 2, :], O, GA, M), 'ma_ready')

            dve.wait_ge(S['cm_mm'], 1)
            link(v.scalar_tensor_tensor(out=CD, in0=ZP[0][:, 0:NCOL].unsqueeze(1).broadcast_to([128, KT, NCOL]),
                                        scalar=-1.0 / D, in1=C, op0=M, op1=AD), 'cd_ready')
            dve.wait_ge(S['cstd_ready'], 1)
            link(v.reciprocal(lnr, lnr), chain)
            dve.wait_ge(S['csq_ready'], 1)
            link(v.tensor_tensor(CD, CD, lnr.unsqueeze(1).broadcast_to([128, KT, NCOL]), M), chain)
            dve.wait_ge(S['cv_mm'], 1)
            for k in range(KT):
                note(v.tensor_scalar(CD[:, k, :], CD[:, k, :], vcol('cln_g', k), vcol('cln_b', k), M, AD), 'cn_ready')
            for k in range(KT):
                dve.wait_ge(S['cs_sig'], k + 1)
                link(v.tensor_tensor(CD[:, k, :], CD[:, k, :], CS[:, k, :], M), chain)
                link(v.tensor_tensor(CD[:, k, :], CD[:, k, :], GB[:, k, :], M), chain)
                link(v.tensor_tensor(MA[:, k, :], MA[:, k, :], CD[:, k, :], AD), 'merged_ready')
            moe_dve(dve, note, link, v)

        @block.gpsimd
        def _(pool):
            note, link = counted(pool)
            gp = nc.gpsimd
            for x in (a_bd, b_bd, k_bd, LT_bd, AK_bd, TT_bd, Y_bd, V_bd, U_bd):
                gp.memset(x, 0.0)
            link(gp.memset(S_bd, 0.0), 'bd_zero')
            pool.wait_ge(S['xn_ready'], 3)
            pool.dma_start(out['shift_p'][0], xrow[127:128, 1, :]).then_inc(S['shift_out'], 16)
            pool.dma_start(out['shift_s'][0], xrow[0:NS, 2, :]).then_inc(S['shift_out'], 16)
            pool.dma_start(out['conv_s'][0][:, 0:CW - 2, :], A['state_conv'][0][:, 1:CW - 1, :]) \
                .then_inc(S['shift_out'], 16)
            conv_state = A['state_conv'][0].rearrange("s w c -> (s w) c").rearrange("(h r) c -> r h c", h=2)

            for g in range(NG):
                cs = slice(256 * g, 256 * g + 256)
                wait(pool, 'tr_mm', 11 * (g - 1) + 4)
                pool.dma_start(SCR[0:120, :, :], conv_state[:, :, cs]).then_inc(scr_in, 16)
                if g:
                    pool.wait_ge(S['samp_out'], 16 * NS * g)
                for s in range(NS):
                    pool.dma_start(SM[16 * s:16 * s + 16].rearrange("p a b -> p (a b)"),
                                   A['state_wkv'][0, s, 4 * g:4 * g + 4].rearrange("h (w v) k -> (h w) (v k)", w=4)) \
                        .then_inc(S['sst_in'], 16)
                pool.wait_ge(S['plain_ready'], 4 * (g + 1))
                for dst, src in ((b_bd, BP), (a_bd, AR[:, :, 0, :]), (k_bd, KP)):
                    for lo, hi in halves:
                        link(gp.tensor_copy(dst[lo:hi, :, lo:hi], src[lo:hi]), 'pbd_ready')
                for q, src in enumerate((LZ[:, 0], DC, LZ[:, 1], LZ[:, 2], KK, AA)):
                    link(gp.tensor_copy(QS[:, :, q, :], src[:, :, NP + 1:NCOL:2]), 'qs_ready')
                pool.wait_ge(S['lmask_ready'], 4 * g + 2)
                for lo, hi in halves:
                    link(gp.tensor_copy(LT_bd[lo:hi, :, lo:hi], X1[lo:hi, :, 0, :]), 'lbd_ready')
                pool.wait_ge(S['tt_ready'], 6 * g + 1)
                link(gp.tensor_copy(TT_bd[64:128, :, 64:128], TT_st[64:128, :, :]), 'ttbd_pool')
                pool.wait_ge(S['lmask_ready'], 4 * g + 4)
                for lo, hi in halves:
                    link(gp.tensor_copy(AK_bd[lo:hi, :, lo:hi], X2[lo:hi, :, 0, :]), 'lbd_ready')
                for i in range(len(LEVELS)):
                    pool.wait_ge(S['y_ready'], 5 * g + i + 1)
                    link(gp.tensor_copy(Y_bd[64:128, :, 64:128], Y_st[64:128, :, :]), 'ybd_pool')
                    pool.wait_ge(S['tt_ready'], 6 * g + i + 2)
                    link(gp.tensor_copy(TT_bd[64:128, :, 64:128], TT_st[64:128, :, :]), 'ttbd_pool')
                    if i == 1:
                        pool.wait_ge(S['tr_free'], 11 * g + 3)
                        pool.dma_start(qd[g], QR[0:48, :]).then_inc(S['qv_sent'], 16)
                    if i == 3:
                        pool.wait_ge(S['qv_sent'], 16 * (g + 1))
                        src = qd[g].rearrange("(q s) (h n) -> (s h) q n", q=6, n=CH)
                        for w in range(4):
                            pool.dma_start(QV[w:128:4, :, :], src).then_inc(S['qv_in'], 16)
                        pool.dma_start(QVV, qd[g][3 * NS:4 * NS, :].rearrange("s (p n) -> (s p) n", n=16)) \
                            .then_inc(S['qv_in'], 16)
                for c in range(NCH):
                    n = NCH * g + c
                    pool.wait_ge(S['ust_ready'], n + 1)
                    for lo, hi in halves:
                        link(gp.tensor_copy(U_bd[lo:hi, :, lo:hi], U_st[lo:hi]), 'ubd_ready')
                    pool.wait_ge(S['s_ready'], n + 1)
                    pool.wait_ge(S['o_mm'], n + 1)
                    for lo, hi in halves:
                        link(gp.tensor_copy(S_bd[lo:hi, :, lo:hi], S_st[lo:hi]), 'sbd_ready')
                pool.wait_ge(S['os_ready'], g + 1)
                pool.dma_start(od[g], OS).then_inc(S['od_out'], 16)
                for s in range(NS):
                    pool.dma_start(out['wkv_s'][0, s, 4 * g:4 * g + 4].rearrange("h (w v) k -> (h w) (v k)", w=4),
                                   SM[16 * s:16 * s + 16].rearrange("p a b -> p (a b)")).then_inc(S['samp_out'], 16)
                pool.wait_ge(S['od_out'], 16 * (g + 1))
                pool.dma_start(OR[0:NS, :], od[g].rearrange("(s p) n -> s (p n)", s=NS)).then_inc(S['os_in'], 16)
                pool.dma_start(out['conv_p'][0, 0, :, cs], UR[0:CW - 1, :]).then_inc(S['conv_out'], 16)
                pool.dma_start(out['conv_s'][0, :, CW - 2, cs], UR[CW:46:2, :]).then_inc(S['conv_out'], 16)
                pool.wait_ge(S['tr_free'], 11 * g + 10)
                for lo, hi in halves:
                    pool.dma_start(out['wkv_p'][0, 0, 4 * g + lo // 64:4 * g + 4:2].rearrange("h v k -> v h k"),
                                   SO[lo:hi, :, lo:hi]).then_inc(S['state_out'], 16)
            pool.wait_ge(S['state_out'], 32 * NG)
            pool.wait_ge(S['conv_out'], 32 * NG)
            pool.wait_ge(S['shift_out'], 48)
            pool.wait_ge(S['samp_out'], 16 * NS * NG)
            moe_pool(pool, note, link, gp)

_INS = ['x_prompt', 'x_sample', 'state_wkv', 'state_shift', 'state_conv', 'norm1_g', 'w_in', 'mu_shift', 'w0',
        'w_decay_up', 'a0', 'a_up', 'g_up', 'k_k', 'k_a', 'r_k', 'gn_g', 'gn_b', 'conv_w', 'conv_b', 'cln_g',
        'cln_b', 'w_out', 'norm2_g', 'w_router', 'e_bias', 'w_gate', 'w_up', 'w_down', 'ws_gate', 'ws_up',
        'ws_down', 'normf_g']
_OUTS = [('y_p', (1, NP, D)), ('y_s', (NS, 1, D)), ('wkv_p', (1, 1, 16, CH, CH)), ('shift_p', (1, 1, D)),
         ('conv_p', (1, 1, CW - 1, D)), ('wkv_s', (1, NS, 16, CH, CH)), ('shift_s', (1, NS, D)),
         ('conv_s', (1, NS, CW - 1, D))]


def kernel(**inputs):
    import concourse.bacc as _bacc
    from concourse.bass_utils import run_bass_kernel_spmd as _run

    nc = _bacc.Bacc("TRN2", target_bir_lowering=False, num_devices=1)
    arrays = {f"in_{n}": np.ascontiguousarray(inputs[n]) for n in _INS}
    arrays["in_const"] = CONST_ARRAY
    A = {n[3:]: nc.dram_tensor(n, a.shape, F32, kind="ExternalInput").ap() for n, a in arrays.items()}
    out = {n: nc.dram_tensor(f"out_{n}", shape, F32, kind="ExternalOutput").ap() for n, shape in _OUTS}
    layer_step(nc, A, out)
    r = _run(nc, [arrays], core_ids=[0])
    return tuple(r.results[0][f"out_{n}"] for n, _ in _OUTS)
```

```python
import numpy as np
from contextlib import ExitStack

import concourse.bass as bass
from concourse import mybir

F32 = mybir.dt.float32
U32 = mybir.dt.uint32
I32 = mybir.dt.int32
ALU = mybir.AluOpType
ACT = mybir.ActivationFunctionType
AX = mybir.AxisListType

D = 1024
NP = 256
NS = 8
NT = NP + NS
NCOL = NP + 2 * NS
KT = D // 128
NG = 4
CH = 64
NCH = NP // CH
NU = 2 * NCH
CW = 31
NE, FE = 64, 256
SLOTS = 64
MAXPASS = (NT + SLOTS - 1) // SLOTS
GN_EPS, LN_EPS, RMS_EPS = 64e-5, 1e-5, 1e-6
EXP_M05 = float(np.exp(-0.5))
LEVELS = (2, 4, 8, 16, 32)

C_R, C_K, C_V, C_LORA = 0, D, 2 * D, 3 * D
C_GLU_A = 3 * D + 256
C_GLU_B = C_GLU_A + D
C_MIX_A = C_GLU_A + 2 * D
C_MIX_B = C_MIX_A + D
GROUP_SECTIONS = (C_R, C_K, C_V, C_GLU_B, C_GLU_A, C_MIX_A, C_MIX_B)
NSEC = len(GROUP_SECTIONS)
NZ = 2 * NSEC

RKV_DONE = [[i for i in range(6) if 12 * c < 8 * i + 8 <= 12 * c + 12] for c in range(4)]

VECS = ('mu_shift', 'w0', 'a0', 'k_k', 'k_a', 'r_k', 'gn_g', 'gn_b', 'conv_b', 'cln_g', 'cln_b')
VROWS = {'mu_shift': 26}
VOFF, _n = {}, 0
for _v in VECS:
    VOFF[_v] = _n
    _n += VROWS.get(_v, KT)
NVEC = _n


def constants():
    p = np.arange(128)
    t = p % 64
    parts = {}
    parts['ident'] = np.eye(128)
    parts['same_head'] = (p[:, None] // 64 == p[None, :] // 64)
    parts['ones'] = np.ones((128, 128))
    s = np.arange(64)
    parts['eye_st'] = (t[:, None] == s[None, :])
    parts['upper'] = np.concatenate([t[:, None] < s[None, :], t[:, None] <= s[None, :]], 1)
    low1 = (t[:, None] // 2 == s[None, :] // 2) & (t[:, None] % 2 == 1) & (s[None, :] % 2 == 0)
    up1 = (t[:, None] // 2 == s[None, :] // 2) & (t[:, None] % 2 == 0) & (s[None, :] % 2 == 1)
    parts['pair_low'], parts['pair_up'] = low1, up1
    for m in LEVELS:
        parts[f'level{m}'] = ((t[:, None] // (2 * m) == s[None, :] // (2 * m))
                              & (t[:, None] // m % 2 == 1) & (s[None, :] // m % 2 == 0))
    parts['before'] = p[:, None] < p[None, :]
    g = np.arange(8)
    parts['lower_group'] = np.tile((g[None, :] < g[:, None]).reshape(1, 64), (128, 1))
    parts['slot'] = np.tile(np.arange(SLOTS * MAXPASS)[None, :], (128, 1))
    parts['dump'] = (NT + p)[:, None]
    parts['token'] = p[:, None] + 128 * np.arange(3)[None, :]
    tok = p[:, None] + 128 * np.arange(3)[None, :]
    parts['row_valid'] = tok < NT
    parts['row_pad'] = tok >= NT
    parts['gn_eps'] = np.full((128, 1), GN_EPS)
    parts['ln_eps'] = np.full((128, 1), LN_EPS)
    parts['rms_eps'] = np.full((128, 1), RMS_EPS)
    off, cols = {}, 0
    for k, v in parts.items():
        off[k] = (cols, cols + v.shape[1])
        cols += v.shape[1]
    return np.concatenate([np.asarray(v, np.float32) for v in parts.values()], 1), off


CONST_ARRAY, CONST_OFF = constants()
NCONST = CONST_ARRAY.shape[1]


def layer_step(nc, A, out, stop=9):
    ctx = ExitStack()
    with ctx:
        def sb(name, shape, dt=F32):
            return ctx.enter_context(nc.sbuf_tensor(name, shape, dt))

        def sem(name):
            return ctx.enter_context(nc.semaphore(name))

        class Arena:
            def __init__(self, base, start, end):
                self.base, self.at, self.end = base, start, end

            def take(self, *dims):
                n = int(np.prod(dims))
                ap = self.base[:, self.at:self.at + n]
                self.at += n
                assert self.at <= self.end, (self.at, self.end)
                names = 'abcd'[:len(dims)]
                if len(dims) > 1:
                    ap = ap.rearrange(f"p ({' '.join(names)}) -> p {' '.join(names)}",
                                      **{names[i]: dims[i] for i in range(len(dims))})
                return ap

        TOTAL = 53200
        big = sb("big", [128, TOTAL])
        keep = Arena(big, 0, TOTAL)
        const = keep.take(NCONST)
        K = {k: const[:, a:b] for k, (a, b) in CONST_OFF.items()}
        ident = K['ident']
        xrow0 = keep.at
        xrow = keep.take(3, D)
        grow = keep.take(D)
        VC = keep.take(NVEC)
        omu = keep.take(26)
        oka = keep.take(KT)
        CWT = keep.take(KT, CW)
        stat = keep.take(16)
        front0 = keep.at
        F = Arena(big, front0, TOTAL)
        C = F.take(KT, NCOL)
        GB = F.take(KT, NCOL)
        MA = F.take(KT, NCOL)
        after_groups0 = F.at
        xT = F.take(KT, NCOL)
        NW = 2
        wring = [F.take(KT, 256) for _ in range(NW)]
        wlora = F.take(D)
        wgate = F.take(D)
        TW = F.take(NCOL)
        SG = F.take(NCOL)
        zs = F.take(2, NCOL + 1)
        LZS = [F.take(3, 2, NCOL), Arena(big, xrow0, front0).take(3, 2, NCOL)]
        DC = F.take(2, NCOL)
        AA = F.take(2, NCOL)
        G = F.take(2, NCOL)
        SB = F.take(2, NCOL)
        GA = F.take(2, NCOL)
        KK = F.take(2, NCOL)
        SQ = F.take(2, NCOL)
        INV = F.take(2, NCOL)
        O = F.take(2, NCOL)
        PP = F.take(2, NCH, CH + 1)
        IP = F.take(2, NCH, CH)
        UU = F.take(2, CW - 1 + NCOL)
        AR = F.take(NU, 2, CH)
        BP = F.take(NU, CH)
        KP = F.take(NU, CH)
        a_bd, b_bd, k_bd = (F.take(NU, 128) for _ in range(3))
        X1 = F.take(NU, 2, CH)
        X2 = F.take(NU, 2, CH)
        LT_bd, AK_bd = (F.take(NU, 128) for _ in range(2))
        T_st, TT_st, Y_st = (F.take(NU, CH) for _ in range(3))
        TT_bd, Y_bd = (F.take(NU, 128) for _ in range(2))
        BT_bd, KTok_bd, V_bd = (F.take(NU, 128) for _ in range(3))
        V_st = F.take(NU, CH)
        Z_st, U_st, S_st = (F.take(2, CH) for _ in range(3))
        U_bd, S_bd, SO = (F.take(2, 128) for _ in range(3))
        QS = F.take(2, 6, NS)
        QR = F.take(256)
        QV = F.take(6, CH)
        SM = F.take(16, CH)
        SMT = F.take(16, CH)
        SA = F.take(16)
        OS = F.take(16)
        OR = F.take(256)
        SCR = F.take(2, 256)
        SCB = F.take(2, NS, CW)
        SCT = F.take(NS, CW)
        UR = F.take(256)
        QVV = F.take(16)
        SCR8 = F.take(NS)
        zero1 = F.take(1)
        VD = SMT.rearrange("p a b -> p (a b)").rearrange("p (u r n) -> p u r n", u=NU, r=2)
        INV2 = O
        flat = lambda x: x.rearrange({3: "p a b -> p (a b)", 4: "p a b c -> p (a b c)"}[len(x.shape)])
        junk, shiftrows, convrows = flat(BT_bd), flat(AR), flat(X1)
        vecrows = flat(X2)[:, 0:128]
        P2 = Arena(big, after_groups0, TOTAL)
        w_out_sb = P2.take(KT, D)
        CD = P2.take(KT, NCOL)
        CS = P2.take(KT, NCOL)
        lnr = P2.take(NCOL)
        hrow_x = P2.take(3, D)

        qd = [nc.dram_tensor(f"qd{g}", (48, 256), F32).ap() for g in range(NG)]
        od = [nc.dram_tensor(f"od{g}", (128, 16), F32).ap() for g in range(NG)]
        ps = [ctx.enter_context(nc.psum_tensor(f"bank{i}", [128, 512], F32)) for i in range(8)]
        ZP, B = ps[0:2], ps[2:8]

        names = """
          small_in consts_in x_in vec_in lora_in wout_in hx_in sst_in qv_in os_in dve_chain act_chain xn_ready
          xt_mm xt_ready vec_mm vec_ready xstd_ready zt_mm z_free_dve z_free_act zs_ready lora_ready lora_mm
          lora_free sq_ready ss_mm root_ready dec_ready plain_ready pbd_ready a_mm lmask_ready lbd_ready
          ltbd_ready tr_mm tr_free y_mm y_ready ybd_act ybd_pool t_mm tt_mm t_ready tt_ready ttbd_act
          ttbd_pool zq_mm zq_ready u_mm ust_ready ubd_ready o_mm o_ready s_mm s_ready sbd_ready state_zero
          state_out qs_ready os_ready conv_out samp_out gm_mm gd_ready gsq_ready gv_mm gstd_ready bo_in bo_mm
          ma_ready shift_out zero_ready c_ready cm_mm cd_ready csq_ready cv_mm cstd_ready cs_sig cn_ready
          merged_ready wo_mm prep_act qv_sent tap sm_ready bd_zero od_out
        """.split()
        S = {n: sem(n) for n in names}
        win_in = [sem(f"win_in{i}") for i in range(NW)]
        scr_in = sem("scr_in")
        globals_ = locals()

        block = ctx.enter_context(nc.Block())

        def counted(eng):
            cnt = {}

            def note(ins, name):
                cnt[name] = cnt.get(name, 0) + 1
                ins.then_inc(S[name], 1)

            def link(ins, name):
                note(ins, name)
                eng.wait_ge(S[name], cnt[name])
            return note, link

        def settle(eng):
            eng.sem_inc(S['passed'], 1)

        def wait(eng, name, k):
            if k > 0:
                eng.wait_ge(S[name], k)

        def z_kind(n):
            if n == 0:
                return 'dve'
            if n == 1:
                return 'dve'
            i = (n - 2) % NZ
            return 'act' if i in (6, 7) or i >= 10 else 'dve'

        def z_wait_free(eng, n):
            if n >= 2:
                kind = z_kind(n - 2)
                eng.wait_ge(S[f'z_free_{kind}'], sum(z_kind(m) == kind for m in range(n - 1)))

        vcol = lambda name, j: VC[:, VOFF[name] + j:VOFF[name] + j + 1]
        mucol = lambda i: VC[:, VOFF['mu_shift'] + i:VOFF['mu_shift'] + i + 1]
        w_in = A['w_in'][0].rearrange("(k p) c -> p k c", p=128)
        halves = ((0, 64), (64, 128))

        PASS = NE * SLOTS
        xg = nc.dram_tensor("xg", (NT, D), F32).ap()
        yrows = nc.dram_tensor("yrows", (MAXPASS * PASS, D), F32).ap()
        NSLOT = 4
        DOWN_FROM = 8
        ring0 = TOTAL - NSLOT * 3 * 2048
        assert P2.at <= ring0, (P2.at, ring0)
        E = Arena(big, front0, ring0)
        x2p = E.take(3, D)
        x2T = E.take(KT, NT)
        hsh = E.take(2, NT)
        sgs = E.take(2, NT)
        wr = E.take(KT, NE)
        ebias = E.take(NE)
        sc, bi, bm, rp, MK = (E.take(3, NE) for _ in range(5))
        m8 = E.take(24, 8)
        gs, gm, gpen = (E.take(3, 8) for _ in range(3))
        G1, G2 = E.take(3, 8, 8), E.take(3, 8, 8)
        m8b = E.take(3, 8)
        den = E.take(3)
        NEP = NE + 4
        gate = E.take(3, NE)
        posm = E.take(3, NEP)
        cntf, cnti = E.take(1), E.take(1).bitcast(I32)
        OH = [E.take(3, SLOTS) for _ in range(2)]
        code, code8, gate8 = E.take(3, NE), E.take(3, 8), E.take(3, 8)
        rowf, rowu = E.take(3, 8), E.take(3, 8).bitcast(U32)
        E8 = E.take(8, NE)
        xeT = [E.take(KT, SLOTS) for _ in range(2)]
        hsg = E.take(2 * SLOTS)
        idxu = E.take(4).bitcast(U32)
        xe = [E.take(D) for _ in range(4)]
        hT = [E.take(2, SLOTS) for _ in range(2)]
        ye = [E.take(D) for _ in range(4)]
        slot_w = []
        for i in range(NSLOT):
            W_ = Arena(big, ring0 + i * 6144, ring0 + (i + 1) * 6144)
            slot_w.append((W_.take(KT, FE), W_.take(KT, FE), W_.take(2, D)))
        back = big[:, ring0:ring0 + 24 * D].rearrange("p (t j d) -> p t j d", t=3, j=8)
        ps_idx, ps_x, ps_h, ps_y = ps[0], ps[1], (ps[2], ps[3]), ((ps[4], ps[5]), (ps[6], ps[7]))

        for n in """wgu_in wd_in""".split():
            for i in range(NSLOT):
                S[f'{n}{i}'] = sem(f'{n}{i}')
        for i in range(4):
            S[f'gath{i}'] = sem(f'gath{i}')
            S[f'y_out{i}'] = sem(f'y_out{i}')
        for i in range(5):
            S[f'back_in{i}'] = sem(f'back_in{i}')
        for n in """
          idx_mm idx_ready xtr_mm x2_out ov_gath passed ov_out code_ready sum_ready ov_pe ov_act ov_dve
          sc_ready2 hsg_ready grow_in wr_in h2_ready h2std_ready x2_ready x2t_mm x2t_ready rt_mm sc_ready
          mk_ready pos_mm cnt_ready shg_mm shs_ready shh_ready shd_mm shy_ready oh_ready xet_ready h_mm
          sig_ready ht_ready yx_mm ye_act ye_dve ov_w fin_std fin_ready fin_out rout_ready
        """.split():
            S[n] = sem(n)

        def load_item(sp, part, slot, src):
            dst = slot_w[slot][part]
            if part < 2:
                ap = src.rearrange("(p k) f -> p k f", k=KT)
            else:
                ap = src.rearrange("(j p) d -> p j d", p=128)
            sp.dma_start(dst, ap).then_inc(S[('wgu_in', 'wgu_in', 'wd_in')[part] + str(slot)], 16)

        def expert_w(part, e):
            name = ('w_gate', 'w_up', 'w_down')[part]
            if isinstance(e, int):
                return A[name][0, e]
            return A[name][0, bass.ds(e, 1)].rearrange("a r c -> (a r) c")

        def moe_sp(sp):
            sp.wait_ge(S['xn_ready'], 3)
            sp.dma_start(grow, A['norm2_g'][0:1, :].partition_broadcast(128)).then_inc(S['grow_in'], 16)
            for part, n in enumerate(('ws_gate', 'ws_up', 'ws_down')):
                load_item(sp, part, 0, A[n][0])
            for e in range(3):
                for part in range(3):
                    load_item(sp, part, e + 1, expert_w(part, e))
            sp.wait_ge(S['h2_ready'], 6)
            sp.dma_start(wr, A['w_router'][0].rearrange("(p k) e -> p k e", k=KT)).then_inc(S['wr_in'], 16)
            sp.dma_start(ebias, A['e_bias'][0:1, :].partition_broadcast(128)).then_inc(S['wr_in'], 16)
            sp.wait_ge(S['x2_ready'], 3)
            sp.dma_start(grow, A['normf_g'].rearrange("(a d) -> a d", a=1).partition_broadcast(128)) \
              .then_inc(S['grow_in'], 16)
            sp.dma_start(xg[0:NP, :].rearrange("(t p) d -> p t d", p=128), x2p[:, 0:2, :]).then_inc(S['x2_out'], 16)
            sp.dma_start(xg[NP:NT, :], x2p[0:NS, 2, :]).then_inc(S['x2_out'], 16)
            sp.wait_ge(S['shg_mm'], 4)
            load_item(sp, 0, 0, expert_w(0, 3))
            load_item(sp, 1, 0, expert_w(1, 3))
            sp.wait_ge(S['shy_ready'], 6)
            load_item(sp, 2, 0, expert_w(2, 3))
            with sp.Fori(1, NE // 4) as i:
                for b in range(4):
                    e = 4 * i + b
                    sp.wait_ge(S['h_mm'], e - 3)
                    load_item(sp, 0, (b + 1) % 4, expert_w(0, e))
                    load_item(sp, 1, (b + 1) % 4, expert_w(1, e))
                    sp.wait_ge(S['yx_mm'], e - 3)
                    load_item(sp, 2, (b + 1) % 4, expert_w(2, e))
            sp.wait_ge(S['cnt_ready'], 1)
            count = sp.value_load(cnti[0:1, 0:1])
            for c in range(1, MAXPASS):
                with sp.If(count > SLOTS * c):
                    if c == 1:
                        sp.wait_ge(S['yx_mm'], NE)
                    with sp.Fori(0, NE) as e:
                        n = (c - 1) * NE + e
                        if c == 1:
                            with sp.If(e > 0):
                                sp.wait_ge(S['ov_pe'], 4 * n)
                                settle(sp)
                        else:
                            sp.wait_ge(S['ov_pe'], 4 * n)
                        for part, name in enumerate(('w_gate', 'w_up', 'w_down')):
                            ap = expert_w(part, e)
                            ap = (ap.rearrange("(p k) f -> p k f", k=KT) if part < 2
                                  else ap.rearrange("(j p) d -> p j d", p=128))
                            sp.dma_start(slot_w[0][part], ap).then_inc(S['ov_w'], 16)
            sp.wait_ge(S['fin_ready'], 3)
            sp.dma_start(out['y_p'][0].rearrange("(t p) d -> p t d", p=128), xrow[:, 0:2, :]).then_inc(S['fin_out'], 16)
            sp.dma_start(out['y_s'][:, 0, :], xrow[0:NS, 2, :]).then_inc(S['fin_out'], 16)
            sp.wait_ge(S['fin_out'], 32)

        TAIL = (0, 2, 1)

        def tile_rows(t):
            return 128 if t < 2 else NS

        def moe_pe(pe, note, mm):
            for t in range(3):
                r = tile_rows(t)
                pe.wait_ge(S['x2_ready'], t + 1)
                for k in range(KT):
                    ins = nc.tensor.transpose(B[2 * t + k // 4][:, 128 * (k % 4):128 * (k % 4) + r],
                                              x2p[0:r, t, 128 * k:128 * k + 128], ident[0:r, 0:r])
                    if k % 4 == 3:
                        note(ins, 'x2t_mm')
            pe.wait_ge(S['x2t_ready'], 6)
            pe.wait_ge(S['wr_in'], 32)
            for t in range(3):
                r = tile_rows(t)
                for k in range(KT):
                    ins = mm(B[5][0:r, 64 * t:64 * t + 64], x2T[:, k, 128 * t:128 * t + r], wr[:, k, :],
                             k == 0, k == KT - 1)
            note(ins, 'rt_mm')
            sw = slot_w[0]
            for j in range(2):
                for part in range(2):
                    if j == 0 and part == 0:
                        pe.wait_ge(S['wgu_in0'], 32)
                    for k in range(KT):
                        ins = mm(ps[2 * part + j][:, 0:NT], sw[part][:, k, 128 * j:128 * j + 128], x2T[:, k, :],
                                 k == 0, k == KT - 1)
                    note(ins, 'shg_mm')
            pe.wait_ge(S['mk_ready'], 1)
            for t in range(3):
                for s in range(t + 1):
                    ins = mm(ps[7][:, 64 * t:64 * t + 64], K['before'] if s == t else K['ones'], MK[:, s, :],
                             s == 0, s == t)
            for s in range(3):
                ins = mm(ps[7][:, 192:256], K['ones'], MK[:, s, :], s == 0, s == 2)
            note(ins, 'pos_mm')
            pe.wait_ge(S['shh_ready'], 2)
            pe.wait_ge(S['wd_in0'], 16)
            for n, (t, h) in enumerate((t, h) for t in range(3) for h in range(2)):
                r = tile_rows(t)
                bank = ps[(4, 5, 6, 1, 2, 3)[n]]
                for j in range(2):
                    ins = mm(bank[0:r, :], hsh[:, j, 128 * t:128 * t + r], sw[2][:, j, 512 * h:512 * h + 512],
                             j == 0, j == 1)
                note(ins, 'shd_mm')

            pe.wait_ge(S['rout_ready'], 1)
            pe.wait_ge(S['shy_ready'], 6)

            def lists(col, oh):
                for t in range(3):
                    r = tile_rows(t)
                    ins = mm(ps_idx[0:SLOTS, col:col + 1], oh[0:r, t, :], K['token'][0:r, t:t + 1], t == 0, t == 2)
                return ins

            def rows_over(x):
                for k in range(KT):
                    ins = nc.tensor.transpose(ps_x[:, SLOTS * k:SLOTS * k + SLOTS],
                                              x[0:SLOTS, 128 * k:128 * k + 128], ident[0:SLOTS, 0:SLOTS])
                return ins

            def index(e, b):
                pe.wait_ge(S['oh_ready'], e + 1)
                if not (isinstance(e, int) and e < 1):
                    pe.wait_ge(S['idx_ready'], e)
                note(lists(b % 4, OH[b % 2]), 'idx_mm')

            def turn(e, b, turns):
                pe.wait_ge(S[f'gath{b % 4}'], 16 * (turns + 1))
                if not (isinstance(e, int) and e < 1):
                    pe.wait_ge(S['xet_ready'], e)
                settle(pe)
                note(rows_over(xe[b % 4]), 'xtr_mm')

            def hidden_products(s, b):
                for part in range(2):
                    for j in range(2):
                        c = SLOTS * (2 * part + j)
                        for k in range(KT):
                            yield mm(ps_h[b % 2][:, c:c + SLOTS], slot_w[s][part][:, k, 128 * j:128 * j + 128],
                                     xeT[b % 2][:, k, :], k == 0, k == KT - 1)

            def down_products(s, b):
                for h in range(2):
                    for c in range(0, 512, 128):
                        for j in range(2):
                            yield mm(ps_y[b % 2][h][0:SLOTS, c:c + 128], hT[b % 2][:, j, :],
                                     slot_w[s][2][:, j, 512 * h + c:512 * h + c + 128], j == 0, j == 1)

            def wait_gate_up(e, i, b):
                pe.wait_ge(S['xet_ready'], e + 1)
                if not (isinstance(e, int) and e < 2):
                    pe.wait_ge(S['ht_ready'], e - 1)
                pe.wait_ge(S[f'wgu_in{(b + 1) % 4}'], 32 * (i + (2 if b == 3 else 1)))

            def wait_down(e, i, b):
                pe.wait_ge(S['ht_ready'], e + 1)
                pe.wait_ge(S[f'wd_in{(b + 1) % 4}'], 16 * (i + (2 if b == 3 else 1)))
                if not (isinstance(e, int) and e < 2):
                    pe.wait_ge(S['ye_act'], e - 1)
                    pe.wait_ge(S['ye_dve'], e - 1)

            def products(e, i, b):
                wait_gate_up(e, i, b)
                first = isinstance(i, int) and b == 0
                downs = iter(()) if first else down_products(b % 4, b + 3)
                for n, ins in enumerate(hidden_products((b + 1) % 4, b)):
                    if n == DOWN_FROM and not first:
                        wait_down(e - 1, i if b else i - 1, (b + 3) % 4)
                    if DOWN_FROM <= n < DOWN_FROM + 16:
                        last_down = next(downs, None)
                note(ins, 'h_mm')
                if not first:
                    note(last_down, 'yx_mm')

            def down(e, i, b):
                wait_down(e, i, b)
                for ins in down_products((b + 1) % 4, b):
                    pass
                note(ins, 'yx_mm')

            def four(i):
                for b in range(4):
                    e = 4 * i + b
                    index(e + 3, b + 3)
                    turn(e + 1, b + 1, i if b < 3 else i + 1)
                    products(e, i, b)

            for e in range(3):
                index(e, e)
            turn(0, 0, 0)
            four(0)
            with pe.Fori(1, NE // 4) as i:
                four(i)
            down(NE - 1, NE // 4 - 1, 3)
            pe.wait_ge(S['cnt_ready'], 1)
            count = pe.value_load(cnti[0:1, 0:1])
            for c in range(1, MAXPASS):
                with pe.If(count > SLOTS * c):
                    if c == 1:
                        pe.wait_ge(S['ye_act'], NE)
                        pe.wait_ge(S['ye_dve'], NE)
                    with pe.Fori(0, NE) as e:
                        n = (c - 1) * NE + e + 1
                        pe.wait_ge(S['ov_dve'], 5 * n - 4)
                        lists(0, OH[0]).then_inc(S['ov_pe'], 1)
                        pe.wait_ge(S['ov_gath'], 16 * n)
                        settle(pe)
                        rows_over(xe[0]).then_inc(S['ov_pe'], 1)
                        pe.wait_ge(S['ov_act'], 3 * n - 2)
                        pe.wait_ge(S['ov_w'], 48 * n)
                        for part in range(2):
                            for j in range(2):
                                cc = SLOTS * (2 * part + j)
                                for k in range(KT):
                                    ins = mm(ps_h[0][:, cc:cc + SLOTS], slot_w[0][part][:, k, 128 * j:128 * j + 128],
                                             xeT[0][:, k, :], k == 0, k == KT - 1)
                        ins.then_inc(S['ov_pe'], 1)
                        pe.wait_ge(S['ov_dve'], 5 * n - 1)
                        for h in range(2):
                            for j in range(2):
                                ins = mm(ps_y[0][h][0:SLOTS, :], hT[0][:, j, :],
                                         slot_w[0][2][:, j, 512 * h:512 * h + 512], j == 0, j == 1)
                        ins.then_inc(S['ov_pe'], 1)

        def moe_act(act, note, link, fn):
            for t in range(3):
                r = tile_rows(t)
                act.wait_ge(S['h2_ready'], 2 * t + 2)
                link(fn(ye[1][0:r, :], xrow[0:r, t, :], ACT.Square, accum_out=stat[0:r, 9 + t:10 + t]), 'act_chain')
                note(fn(stat[0:r, 12 + t:13 + t], stat[0:r, 9 + t:10 + t], ACT.Sqrt, scale=1.0 / D,
                        bias=K['rms_eps'][0:r, :]), 'h2std_ready')
            for t in range(3):
                r = tile_rows(t)
                for h in range(2):
                    act.wait_ge(S['x2t_mm'], 2 * t + h + 1)
                    note(fn(x2T[:, 4 * h:4 * h + 4, 128 * t:128 * t + r],
                            B[2 * t + h][:, :].rearrange("p (k c) -> p k c", k=4)[:, :, 0:r], ACT.Copy), 'x2t_ready')
            act.wait_ge(S['rt_mm'], 1)
            act.wait_ge(S['sc_ready'], 1)
            for t in range(3):
                r = tile_rows(t)
                note(fn(sc[0:r, t, :], B[5][0:r, 64 * t:64 * t + 64], ACT.Sigmoid), 'sc_ready2')
            for j in range(2):
                act.wait_ge(S['shg_mm'], 2 * j + 1)
                note(fn(sgs[:, j, :], ps[j][:, 0:NT], ACT.Sigmoid), 'shs_ready')

            def turned(e, b):
                act.wait_ge(S['xtr_mm'], e + 1)
                if not (isinstance(e, int) and e < 2):
                    act.wait_ge(S['h_mm'], e - 1)
                note(fn(xeT[b % 2].rearrange("p k n -> p (k n)"), ps_x[:, 0:KT * SLOTS], ACT.Copy), 'xet_ready')

            def sigma(e, b):
                act.wait_ge(S['h_mm'], e + 1)
                if not (isinstance(e, int) and e < 1):
                    act.wait_ge(S['ht_ready'], e)
                note(fn(hsg, ps_h[b % 2][:, 0:2 * SLOTS], ACT.Sigmoid), 'sig_ready')

            def store(e, b, turns):
                act.wait_ge(S['yx_mm'], e + 1)
                if not (isinstance(turns, int) and turns < 1):
                    act.wait_ge(S[f'y_out{b % 4}'], 16 * turns)
                note(fn(ye[b % 4][0:SLOTS, 0:512], ps_y[b % 2][0][0:SLOTS, :], ACT.Copy), 'ye_act')
                act.wait_ge(S['ye_act'], e + 1)
                act.wait_ge(S['ye_dve'], e + 1)
                act.dma_start(yrows[bass.ds(e * SLOTS, SLOTS), :], ye[b % 4][0:SLOTS, :]) \
                    .then_inc(S[f'y_out{b % 4}'], 16)

            def four(i):
                for b in range(4):
                    e = 4 * i + b
                    turned(e + 1, b + 1)
                    sigma(e, b)
                    if b:
                        store(e - 1, b - 1, i)
                    elif not (isinstance(i, int) and i < 1):
                        store(e - 1, 3, i - 1)

            turned(0, 0)
            four(0)
            four(1)
            with act.Fori(2, NE // 4) as i:
                four(i)
            store(NE - 1, 3, NE // 4 - 1)
            act.wait_ge(S['cnt_ready'], 1)
            count = act.value_load(cnti[0:1, 0:1])
            for c in range(1, MAXPASS):
                with act.If(count > SLOTS * c):
                    if c == 1:
                        act.wait_ge(S['y_out0'], 16 * (NE // 4))
                    with act.Fori(0, NE) as e:
                        n = (c - 1) * NE + e + 1
                        act.wait_ge(S['ov_pe'], 4 * n - 2)
                        fn(xeT[0].rearrange("p k n -> p (k n)"), ps_x[:, 0:KT * SLOTS], ACT.Copy) \
                            .then_inc(S['ov_act'], 1)
                        act.wait_ge(S['ov_pe'], 4 * n - 1)
                        fn(hsg, ps_h[0][:, 0:2 * SLOTS], ACT.Sigmoid).then_inc(S['ov_act'], 1)
                        act.wait_ge(S['ov_pe'], 4 * n)
                        fn(ye[0][0:SLOTS, 0:512], ps_y[0][0][0:SLOTS, :], ACT.Copy).then_inc(S['ov_act'], 1)
                        act.wait_ge(S['ov_act'], 3 * n)
                        act.wait_ge(S['ov_dve'], 5 * n)
                        act.dma_start(yrows[bass.ds(e * SLOTS + PASS * c, SLOTS), :], ye[0][0:SLOTS, :]) \
                            .then_inc(S['ov_out'], 16)
                        act.wait_ge(S['ov_out'], 16 * n)
            for n, t in enumerate(TAIL):
                r = tile_rows(t)
                act.wait_ge(S['sum_ready'], n + 1)
                link(fn(x2p[0:r, t, :], xrow[0:r, t, :], ACT.Square, accum_out=stat[0:r, t:t + 1]), 'act_chain')
                note(fn(stat[0:r, 3 + t:4 + t], stat[0:r, t:t + 1], ACT.Sqrt, scale=1.0 / D,
                        bias=K['rms_eps'][0:r, :]), 'fin_std')

        def moe_dve(dve, note, link, v):
            M, AD = ALU.mult, ALU.add
            chain = 'dve_chain'
            dve.wait_ge(S['wo_mm'], 1)
            dve.wait_ge(S['hx_in'], 32)
            dve.wait_ge(S['shift_out'], 48)
            for t in range(3):
                r = tile_rows(t)
                for h in range(2):
                    note(v.tensor_tensor(xrow[0:r, t, 512 * h:512 * h + 512], B[2 * t + h][0:r, :],
                                         hrow_x[0:r, t, 512 * h:512 * h + 512], AD), 'h2_ready')
            v.memset(sc, 0.0)
            link(v.memset(posm[:, :, NE:NEP], 1e6), 'sc_ready')
            dve.wait_ge(S['grow_in'], 16)
            dve.wait_ge(S['h2_ready'], 6)
            for t in range(3):
                r = tile_rows(t)
                dve.wait_ge(S['h2std_ready'], t + 1)
                link(v.reciprocal(stat[0:r, 6 + t:7 + t], stat[0:r, 12 + t:13 + t]), chain)
                link(v.scalar_tensor_tensor(
                    out=x2p[0:r, t, :].rearrange("q (k p) -> q p k", k=KT),
                    in0=xrow[0:r, t, :].rearrange("q (p k) -> q p k", k=KT), scalar=stat[0:r, 6 + t:7 + t],
                    in1=grow[0:r, :].rearrange("q (p k) -> q p k", k=KT), op0=M, op1=M), 'x2_ready')
            dve.wait_ge(S['wr_in'], 32)
            dve.wait_ge(S['sc_ready2'], 3)
            link(v.tensor_tensor(bi, sc, ebias.unsqueeze(1).broadcast_to([128, 3, NE]), AD), chain)
            for t in range(3):
                for q in range(8):
                    ins = v.max(out=m8[:, 8 * t + q, :], in_=bi[:, t, 8 * q:8 * q + 8])
            link(ins, chain)
            link(v.tensor_tensor(gs.rearrange("p t g -> p (t g)"), m8[:, :, 0], m8[:, :, 1], AD), chain)
            other = gs.unsqueeze(2).broadcast_to([128, 3, 8, 8])
            own = gs.unsqueeze(3).broadcast_to([128, 3, 8, 8])
            link(v.tensor_tensor(G2, other, own, ALU.is_equal), chain)
            link(v.tensor_tensor(G2.rearrange("p t a b -> p t (a b)"), G2.rearrange("p t a b -> p t (a b)"),
                                 K['lower_group'].unsqueeze(1).broadcast_to([128, 3, 64]), M), chain)
            link(v.tensor_tensor(G1, other, own, ALU.is_gt), chain)
            link(v.tensor_tensor(G1, G1, G2, AD), chain)
            link(v.tensor_reduce(gm, G1, AX.X, AD), chain)
            link(v.tensor_scalar(gm, gm, 3.5, None, ALU.is_lt), chain)
            link(v.tensor_scalar(gpen, gm, 1e30, -1e30, M, AD), chain)
            by_group = lambda x: x.rearrange("p t (g c) -> p t g c", g=8)
            wide = lambda x: x.unsqueeze(3).broadcast_to([128, 3, 8, 8])
            link(v.tensor_tensor(by_group(bm), by_group(bi), wide(gm), M), chain)
            link(v.tensor_tensor(by_group(bm), by_group(bm), wide(gpen), AD), chain)
            for t in range(3):
                link(v.max(out=m8b[:, t, :], in_=bm[:, t, :]), chain)
                link(v.match_replace(out=rp[:, t, :], in_to_replace=m8b[:, t, :], in_values=bm[:, t, :],
                                     imm_value=-3e38), chain)
            link(v.tensor_scalar(MK, rp, -2e38, None, ALU.is_lt), chain)
            link(v.tensor_tensor(MK, MK, K['row_valid'].unsqueeze(2).broadcast_to([128, 3, NE]), M), 'mk_ready')
            link(v.tensor_tensor(rp, sc, MK, M), chain)
            link(v.tensor_reduce(den, rp, AX.X, AD), chain)
            link(v.tensor_tensor(den, den, K['row_pad'], AD), chain)
            link(v.reciprocal(den, den), chain)
            link(v.tensor_scalar(den, den, 2.5, None, M), chain)
            link(v.tensor_tensor(gate, rp, den.unsqueeze(2).broadcast_to([128, 3, NE]), M), chain)
            link(v.tensor_scalar(bm, MK, -1e6, 1e6, M, AD), chain)
            dve.wait_ge(S['pos_mm'], 1)
            link(v.tensor_tensor(posm[:, :, 0:NE], bm, ps[7][:, 0:192].rearrange("p (t e) -> p t e", t=3), AD),
                 'rout_ready')
            link(v.tensor_reduce(cntf, ps[7][:, 192:256], AX.X, ALU.max), chain)
            link(v.tensor_copy(cnti, cntf), 'cnt_ready')

            def onehot(e, b):
                if not (isinstance(e, int) and e < 2):
                    dve.wait_ge(S['idx_mm'], e - 1)
                col = posm[:, :, e:e + 1] if isinstance(e, int) else posm[:, :, bass.ds(e, 1)]
                note(v.tensor_tensor(OH[b % 2], K['slot'][:, 0:SLOTS].unsqueeze(1).broadcast_to([128, 3, SLOTS]),
                                     col.broadcast_to([128, 3, SLOTS]), ALU.is_equal), 'oh_ready')

            def fetch_rows(e, b):
                dve.wait_ge(S['idx_mm'], e + 1)
                if not (isinstance(e, int) and e < 4):
                    dve.wait_ge(S['xtr_mm'], e - 3)
                note(v.tensor_copy(idxu[0:SLOTS, b % 4:b % 4 + 1], ps_idx[0:SLOTS, b % 4:b % 4 + 1]), 'idx_ready')

            onehot(0, 0)
            onehot(1, 1)
            for j in range(2):
                dve.wait_ge(S['shs_ready'], j + 1)
                link(v.tensor_tensor(sgs[:, j, :], sgs[:, j, :], ps[j][:, 0:NT], M), chain)
                dve.wait_ge(S['shg_mm'], 2 * j + 2)
                note(v.tensor_tensor(hsh[:, j, :], sgs[:, j, :], ps[2 + j][:, 0:NT], M), 'shh_ready')
            for n, (t, h) in enumerate((t, h) for t in range(3) for h in range(2)):
                r = tile_rows(t)
                dve.wait_ge(S['shd_mm'], n + 1)
                x = xrow[0:r, t, 512 * h:512 * h + 512]
                note(v.tensor_tensor(x, x, ps[(4, 5, 6, 1, 2, 3)[n]][0:r, :], AD), 'shy_ready')

            def hidden(e, b):
                dve.wait_ge(S['sig_ready'], e + 1)
                if not (isinstance(e, int) and e < 2):
                    dve.wait_ge(S['yx_mm'], e - 1)
                note(v.tensor_tensor(hsg, hsg, ps_h[b % 2][:, 0:2 * SLOTS], M), 'hsg_ready')
                dve.wait_ge(S['hsg_ready'], e + 1)
                note(v.tensor_tensor(hT[b % 2].rearrange("p j n -> p (j n)"), hsg,
                                     ps_h[b % 2][:, 2 * SLOTS:4 * SLOTS], M), 'ht_ready')

            def take(e, b, turns):
                dve.wait_ge(S['yx_mm'], e + 1)
                if not (isinstance(turns, int) and turns < 1):
                    dve.wait_ge(S[f'y_out{b % 4}'], 16 * turns)
                note(v.tensor_copy(ye[b % 4][0:SLOTS, 512:1024], ps_y[b % 2][1][0:SLOTS, :]), 'ye_dve')

            def four(i):
                for b in range(4):
                    e = 4 * i + b
                    fetch_rows(e + 3, b + 3)
                    onehot(e + 4, b + 4)
                    hidden(e, b)
                    if b:
                        take(e - 1, b - 1, i)
                    elif not (isinstance(i, int) and i < 1):
                        take(e - 1, 3, i - 1)

            for e in range(2):
                fetch_rows(e, e)
                onehot(e + 2, e + 2)
            fetch_rows(2, 2)
            four(0)
            for t in range(3):
                link(v.tensor_scalar(code[:, t, :], K['slot'][:, 0:NE], float(SLOTS), 1.0, M, AD), chain)
            link(v.tensor_tensor(code, code, posm[:, :, 0:NE], AD), chain)
            for c in range(1, MAXPASS):
                link(v.tensor_scalar(sc, posm[:, :, 0:NE], float(SLOTS * c), float(PASS - SLOTS), ALU.is_ge, M), chain)
                link(v.tensor_tensor(code, code, sc, AD), chain)
            link(v.tensor_tensor(code, code, MK, M), chain)
            for t in range(3):
                link(v.max(out=code8[:, t, :], in_=code[:, t, :]), chain)
                link(v.tensor_tensor(E8, code[:, t, :].unsqueeze(1).broadcast_to([128, 8, NE]),
                                     code8[:, t, :].unsqueeze(2).broadcast_to([128, 8, NE]), ALU.is_equal), chain)
                link(v.tensor_tensor(E8, E8, gate[:, t, :].unsqueeze(1).broadcast_to([128, 8, NE]), M), chain)
                link(v.tensor_reduce(gate8[:, t, :], E8, AX.X, AD), chain)
            link(v.tensor_scalar(rowf, code8, -1.0, None, AD), chain)
            link(v.tensor_copy(rowu, rowf), 'code_ready')
            four(1)
            with dve.Fori(2, NE // 4) as i:
                four(i)
            take(NE - 1, 3, NE // 4 - 1)
            count = dve.value_load(cnti[0:1, 0:1])
            for c in range(1, MAXPASS):
                with dve.If(count > SLOTS * c):
                    if c == 1:
                        dve.wait_ge(S['idx_mm'], NE + 3)
                        dve.wait_ge(S['gath0'], 16 * (NE // 4 + 1))
                        dve.wait_ge(S['y_out0'], 16 * (NE // 4))
                    with dve.Fori(0, NE) as e:
                        n = (c - 1) * NE + e + 1
                        v.tensor_tensor(OH[0], K['slot'][:, SLOTS * c:SLOTS * c + SLOTS].unsqueeze(1)
                                        .broadcast_to([128, 3, SLOTS]),
                                        posm[:, :, bass.ds(e, 1)].broadcast_to([128, 3, SLOTS]),
                                        ALU.is_equal).then_inc(S['ov_dve'], 1)
                        dve.wait_ge(S['ov_pe'], 4 * n - 3)
                        v.tensor_copy(idxu[0:SLOTS, 0:1], ps_idx[0:SLOTS, 0:1]).then_inc(S['ov_dve'], 1)
                        dve.wait_ge(S['ov_act'], 3 * n - 1)
                        v.tensor_tensor(hsg, hsg, ps_h[0][:, 0:2 * SLOTS], M).then_inc(S['ov_dve'], 1)
                        dve.wait_ge(S['ov_dve'], 5 * n - 2)
                        v.tensor_tensor(hT[0].rearrange("p j n -> p (j n)"), hsg, ps_h[0][:, 2 * SLOTS:4 * SLOTS], M) \
                            .then_inc(S['ov_dve'], 1)
                        dve.wait_ge(S['ov_pe'], 4 * n)
                        v.tensor_copy(ye[0][0:SLOTS, 512:1024], ps_y[0][1][0:SLOTS, :]).then_inc(S['ov_dve'], 1)
                        dve.wait_ge(S['ov_out'], 16 * n)
            dve.wait_ge(S['grow_in'], 32)
            q = 0

            def finish(n, t):
                r = tile_rows(t)
                dve.wait_ge(S['fin_std'], n + 1)
                link(v.reciprocal(stat[0:r, 6 + t:7 + t], stat[0:r, 3 + t:4 + t]), chain)
                note(v.scalar_tensor_tensor(out=xrow[0:r, t, :], in0=xrow[0:r, t, :], scalar=stat[0:r, 6 + t:7 + t],
                                            in1=grow[0:r, :], op0=M, op1=M), 'fin_ready')

            for n, t in enumerate(TAIL):
                r = tile_rows(t)
                for j in range(8):
                    if j == 0 or (j == 4 and t < 2):
                        dve.wait_ge(S[f'back_in{q}'], 64 if t < 2 else 128)
                        q += 1
                    link(v.scalar_tensor_tensor(out=xrow[0:r, t, :], in0=back[0:r, t, j, :], scalar=gate8[0:r, t, j:j + 1],
                                                in1=xrow[0:r, t, :], op0=M, op1=AD), chain if j < 7 else 'sum_ready')
                if n:
                    finish(n - 1, TAIL[n - 1])
            finish(2, TAIL[2])

        def moe_pool(pool):
            def fetch(x, col, sem_name):
                pool.indirect_dma_start(out=x[0:SLOTS, :], out_offset=None, in_=xg,
                                        in_offset=bass.IndirectOffsetOnAxis(ap=idxu[0:SLOTS, col:col + 1], axis=0)) \
                    .then_inc(S[sem_name], 16)

            def gather(e, b):
                pool.wait_ge(S['idx_ready'], e + 1)
                if not (isinstance(e, int) and e < 4):
                    pool.wait_ge(S['xtr_mm'], e - 3)
                settle(pool)
                fetch(xe[b % 4], b % 4, f'gath{b % 4}')

            pool.wait_ge(S['x2_out'], 32)
            for e in range(6):
                gather(e, e)
            with pool.Fori(1, NE // 4) as i:
                for b in range(4):
                    gather(4 * i + b + 2, b + 2)
            gather(NE + 2, NE + 2)
            pool.wait_ge(S['code_ready'], 1)
            for b in range(4):
                pool.wait_ge(S[f'y_out{b}'], 16 * (NE // 4))
            pool.wait_ge(S['cnt_ready'], 1)
            count = pool.value_load(cnti[0:1, 0:1])
            with pool.If(count > SLOTS):
                for c in range(1, MAXPASS):
                    with pool.If(count > SLOTS * c):
                        with pool.Fori(0, NE) as e:
                            n = (c - 1) * NE + e + 1
                            pool.wait_ge(S['ov_dve'], 5 * n - 3)
                            settle(pool)
                            fetch(xe[0], 0, 'ov_gath')
            for c in range(MAXPASS):
                with pool.If(count > SLOTS * c):
                    with pool.If(count < SLOTS * (c + 1) + 1):
                        if c:
                            pool.wait_ge(S['ov_out'], 16 * NE * c)
                        q = -1
                        for t in TAIL:
                            r = tile_rows(t)
                            for j in range(8):
                                if j == 0 or (j == 4 and t < 2):
                                    q += 1
                                pool.indirect_dma_start(
                                    out=back[0:r, t, j, :], out_offset=None, in_=yrows[0:PASS * (c + 1), :],
                                    in_offset=bass.IndirectOffsetOnAxis(ap=rowu[0:r, t, j:j + 1], axis=0)) \
                                    .then_inc(S[f'back_in{q}'], 16)

        @block.sync
        def _(sp):
            sp.dma_start(const, A['const']).then_inc(S['consts_in'], 16)
            sp.dma_start(xrow[:, 0:2, :], A['x_prompt'][0].rearrange("(t p) d -> p t d", p=128)) \
              .then_inc(S['x_in'], 16)
            sp.dma_start(xrow[0:NS, 2, :], A['x_sample'][:, 0, :]).then_inc(S['small_in'], 16)
            sp.dma_start(shiftrows[0:NS, :], A['state_shift'][0]).then_inc(S['small_in'], 16)
            sp.dma_start(grow, A['norm1_g'][0:1, :].partition_broadcast(128)).then_inc(S['small_in'], 16)
            n = 0
            for v in VECS:
                r = VROWS.get(v, KT)
                src = A[v].rearrange("a h n -> a (h n)") if v == 'r_k' else A[v]
                sp.dma_start(vecrows[n:n + r, :], src[0].rearrange("(r c) -> r c", c=128)) \
                  .then_inc(S['vec_in'], 16)
                n += r
            sp.dma_start(convrows[0:CW, :], A['conv_w'][0]).then_inc(S['vec_in'], 16)
            conv_state = A['state_conv'][0].rearrange("s w c -> (s w) c").rearrange("(h r) c -> r h c", h=2)

            def state_rows(x, s, g):
                return x[0, s, 4 * g:4 * g + 4].rearrange("h (w v) k -> (h w) (v k)", w=4)

            def sample_states(g):
                for s in range(NS):
                    sp.dma_start(SM[16 * s:16 * s + 16].rearrange("p a b -> p (a b)"),
                                 state_rows(A['state_wkv'], s, g)).then_inc(S['sst_in'], 16)

                sp.dma_start(SCR[0:120, :, :], conv_state[:, :, 256 * g:256 * g + 256]).then_inc(scr_in, 16)

            def sample_vectors(g):
                sp.wait_ge(S['tr_free'], 11 * g + 3)
                sp.dma_start(qd[g], QR[0:48, :]).then_inc(S['qv_sent'], 16)
                sp.wait_ge(S['qv_sent'], 16 * (g + 1))
                src = qd[g].rearrange("(q s) (h n) -> (s h) q n", q=6, n=CH)
                for w in range(4):
                    sp.dma_start(QV[w:128:4, :, :], src).then_inc(S['qv_in'], 16)
                sp.dma_start(QVV, qd[g][3 * NS:4 * NS, :].rearrange("s (p n) -> (s p) n", n=16)) \
                    .then_inc(S['qv_in'], 16)

            def after_sample_step(g):
                sp.wait_ge(S['os_ready'], g + 1)
                sp.dma_start(od[g], OS).then_inc(S['od_out'], 16)
                sp.wait_ge(S['od_out'], 16 * (g + 1))
                sp.dma_start(OR[0:NS, :], od[g].rearrange("(s p) n -> s (p n)", s=NS)).then_inc(S['os_in'], 16)

            def after_group(g):
                for s in range(NS):
                    sp.dma_start(state_rows(out['wkv_s'], s, g),
                                 SM[16 * s:16 * s + 16].rearrange("p a b -> p (a b)")).then_inc(S['samp_out'], 16)
                cs = slice(256 * g, 256 * g + 256)
                sp.wait_ge(S['tr_free'], 11 * g + 9)
                sp.dma_start(out['conv_p'][0, 0, :, cs], UR[0:CW - 1, :]).then_inc(S['conv_out'], 16)
                sp.dma_start(out['conv_s'][0, :, CW - 2, cs], UR[CW:46:2, :]).then_inc(S['conv_out'], 16)
                if g + 1 < NG:
                    sp.wait_ge(S['samp_out'], 16 * NS * (g + 1))
                    sample_states(g + 1)
                sp.wait_ge(S['tr_free'], 11 * g + 10)
                for lo, hi in halves:
                    sp.dma_start(out['wkv_p'][0, 0, 4 * g + lo // 64:4 * g + 4:2].rearrange("h v k -> v h k"),
                                 SO[lo:hi, :, lo:hi]).then_inc(S['state_out'], 16)

            for q in range(1 + NSEC * NG):
                c0 = C_LORA if q == 0 else GROUP_SECTIONS[(q - 1) % NSEC] + 256 * ((q - 1) // NSEC)
                if q >= NW:
                    sp.wait_ge(S['zt_mm'], 2 * (q - NW) + 2)
                sp.dma_start(wring[q % NW], w_in[:, :, c0:c0 + 256]).then_inc(win_in[q % NW], 16)
                if q == 1:
                    sp.dma_start(wlora[0:64, :], A['w_decay_up'][0]).then_inc(S['lora_in'], 16)
                    sp.dma_start(wlora[64:128, :], A['a_up'][0]).then_inc(S['lora_in'], 16)
                    sp.dma_start(wgate, A['g_up'][0]).then_inc(S['lora_in'], 16)
                    sample_states(0)
                g, rest = divmod(q - NW - 1, NSEC)
                if g >= 0 and rest == NSEC - 1:
                    sample_vectors(g)
                if g >= 1 and rest == 1:
                    after_sample_step(g - 1)
                if g >= 1 and rest == 2:
                    after_group(g - 1)
            sample_vectors(NG - 1)
            after_sample_step(NG - 1)
            after_group(NG - 1)
            sp.wait_ge(S['ma_ready'], NG)
            sp.wait_ge(S['c_ready'], NG)
            sp.wait_ge(S['state_out'], 16 * 2 * NG)
            sp.wait_ge(S['conv_out'], 16 * 2 * NG)
            sp.wait_ge(S['samp_out'], 16 * NS * NG)
            for h in range(2):
                sp.dma_start(w_out_sb[:, :, 512 * h:512 * h + 512],
                             A['w_out'][0].rearrange("(k p) c -> p k c", p=128)[:, :, 512 * h:512 * h + 512]) \
                  .then_inc(S['wout_in'], 16)
            sp.dma_start(hrow_x[:, 0:2, :], A['x_prompt'][0].rearrange("(t p) d -> p t d", p=128)) \
              .then_inc(S['hx_in'], 16)
            sp.dma_start(hrow_x[0:NS, 2, :], A['x_sample'][:, 0, :]).then_inc(S['hx_in'], 16)
            moe_sp(sp)

        @block.tensor
        def _(pe):
            note, link = counted(pe)

            def mm(out_, lhsT, rhs, start=True, stop=True):
                return nc.tensor.matmul(out_, lhsT=lhsT, rhs=rhs, start=start, stop=stop)

            pe.wait_ge(S['consts_in'], 16)
            for t in range(2):
                pe.wait_ge(S['xn_ready'], t + 1)
                for k in range(KT):
                    ins = nc.tensor.transpose(B[2 * t + k // 4][:, 128 * (k % 4):128 * (k % 4) + 128],
                                              xrow[:, t, 128 * k:128 * k + 128], ident)
                    if k % 4 == 3:
                        note(ins, 'xt_mm')
            pe.wait_ge(S['xn_ready'], 3)
            pe.wait_ge(S['small_in'], 48)
            for k in range(KT):
                nc.tensor.transpose(B[4][:, 16 * k:16 * k + 8], xrow[0:NS, 2, 128 * k:128 * k + 128],
                                    ident[0:NS, 0:NS])
                ins = nc.tensor.transpose(B[4][:, 16 * k + 8:16 * k + 16], shiftrows[0:NS, 128 * k:128 * k + 128],
                                          ident[0:NS, 0:NS])
            note(ins, 'xt_mm')
            pe.wait_ge(S['vec_in'], 16 * (len(VECS) + 1))
            nc.tensor.transpose(B[5][:, 0:NVEC], vecrows[0:NVEC, :], ident[0:NVEC, 0:NVEC])
            for k in range(KT):
                ins = nc.tensor.transpose(B[5][:, 128 + CW * k:128 + CW * k + CW],
                                          convrows[0:CW, 128 * k:128 * k + 128], ident[0:CW, 0:CW])
            note(ins, 'vec_mm')

            def z_tile(n, k0=0, k1=KT):
                q = n // 2
                if k0 == 0:
                    if n % 2 == 0:
                        pe.wait_ge(win_in[q % NW], 16 * (q // NW + 1))
                    z_wait_free(pe, n)
                for k in range(k0, k1):
                    ins = mm(ZP[n % 2][:, 0:NCOL], wring[q % NW][:, k, 128 * (n % 2):128 * (n % 2) + 128],
                             xT[:, k, :], k == 0, k == KT - 1)
                if k1 == KT:
                    note(ins, 'zt_mm')

            def rkv_of_next(g, step):
                if g + 1 < NG:
                    at, end = 3 * step, 3 * step + 3
                    while at < end:
                        k0 = at % KT
                        k1 = min(KT, k0 + end - at)
                        z_tile(2 + NZ * (g + 1) + at // KT, k0, k1)
                        at += k1 - k0

            pe.wait_ge(S['xt_ready'], 6)
            z_tile(0)
            z_tile(1)
            pe.wait_ge(S['lora_in'], 48)
            pe.wait_ge(S['lora_ready'], 3)
            for n in range(2, 12):
                z_tile(n)
            ring = [0]

            for g in range(NG):
                z0 = 2 + NZ * g

                def ring_bank():
                    i = ring[0]
                    ring[0] += 1
                    wait(pe, 'tr_free', i - 2)
                    return B[(1, 4, 5)[i % 3]]

                wait(pe, 'gd_ready', g)
                wait(pe, 'gstd_ready', 2 * g)
                if g == 0:
                    pe.wait_ge(S['vec_ready'], 2)
                for p in range(2):
                    c = slice(256 * g + 128 * p, 256 * g + 128 * p + 128)
                    note(mm(B[p][:, 0:NCOL], wlora[0:64, c], TW[0:64, :]), 'lora_mm')
                for p in range(2):
                    c = slice(256 * g + 128 * p, 256 * g + 128 * p + 128)
                    note(mm(B[2 + p][:, 0:NCOL], wlora[64:128, c], TW[64:128, :]), 'lora_mm')
                pe.wait_ge(S['sq_ready'], g + 1)
                pe.wait_ge(S['lora_free'], 6 * g + 2)
                for p in range(2):
                    note(mm(B[p][:, 0:NCOL], K['same_head'], SQ[:, p, :]), 'ss_mm')
                wait(pe, 'ma_ready', g)
                for p in range(2):
                    c = slice(256 * g + 128 * p, 256 * g + 128 * p + 128)
                    note(mm(B[4 + p][:, 0:NCOL], wgate[:, c], SG), 'lora_mm')
                for i in range(10, 14):
                    z_tile(z0 + i)
                pe.wait_ge(S['lora_free'], 6 * (g + 1))
                pe.wait_ge(S['plain_ready'], 4 * (g + 1))
                pe.wait_ge(S['pbd_ready'], 6 * (g + 1))
                pe.wait_ge(S['root_ready'], 2 * (g + 1))
                arf = AR.rearrange("p u w n -> p u (w n)")
                for h in range(2):
                    for u in range(4 * h, 4 * h + 4):
                        ins = mm(B[2 + h][:, 128 * (u % 4):128 * (u % 4) + 128], b_bd[:, u, :], arf[:, u, :])
                    note(ins, 'a_mm')
                for u in range(NU):
                    ins = mm(B[0][:, CH * u:CH * u + CH], a_bd[:, u, :], BP[:, u, :])
                note(ins, 'a_mm')
                for h in range(2):
                    for u in range(4 * h, 4 * h + 4):
                        ins = mm(B[4 + h][:, 128 * (u % 4):128 * (u % 4) + 128], k_bd[:, u, :], arf[:, u, :])
                    note(ins, 'a_mm')
                pe.wait_ge(S['lmask_ready'], 4 * (g + 1))

                def tr_units(src, h):
                    bank = ring_bank()
                    for u in range(4 * h, 4 * h + 4):
                        ins = nc.tensor.transpose(bank[:, 128 * (u % 4):128 * (u % 4) + 128], src[:, u, :], ident)
                    note(ins, 'tr_mm')

                def tr_v(p):
                    bank = ring_bank()
                    for c in range(NCH):
                        ins = nc.tensor.transpose(
                            bank[:, 128 * c:128 * c + 128],
                            VD[:, NCH * p + c, :, :].rearrange("p r n -> p (r n)"), ident)
                    note(ins, 'tr_mm')

                def tr_samples():
                    bank = ring_bank()
                    for p in range(2):
                        ins = nc.tensor.transpose(bank[0:48, 128 * p:128 * p + 128],
                                                  QS[:, p, :, :].rearrange("p q s -> p (q s)"), ident)
                    note(ins, 'tr_mm')

                def tr_conv_state():
                    pe.wait_ge(scr_in, 16 * (g + 1))
                    bank = ring_bank()
                    for p in range(2):
                        for h in range(2):
                            ins = nc.tensor.transpose(bank[:, 240 * p + 120 * h:240 * p + 120 * h + 120],
                                                      SCR[0:120, h, 128 * p:128 * p + 128], ident[0:120, 0:120])
                    note(ins, 'tr_mm')

                def tr_new_conv():
                    bank = ring_bank()
                    for p in range(2):
                        ins = nc.tensor.transpose(bank[0:46, 128 * p:128 * p + 128], UU[:, p, 256:302], ident)
                    note(ins, 'tr_mm')

                between = [
                    lambda: (tr_units(b_bd, 0), tr_units(b_bd, 1), tr_samples(), tr_conv_state()),
                    lambda: (tr_units(k_bd, 0), tr_units(k_bd, 1)),
                    lambda: (tr_v(0), tr_v(1)),
                    lambda: tr_new_conv(),
                    lambda: None,
                ]
                pe.wait_ge(S['ltbd_ready'], 2 * (g + 1))
                pe.wait_ge(S['lbd_ready'], 2 * (g + 1))
                pe.wait_ge(S['qs_ready'], 6 * (g + 1))
                pe.wait_ge(S['prep_act'], 4 * (g + 1))
                for i, m in enumerate(LEVELS):
                    last = i == len(LEVELS) - 1
                    pe.wait_ge(S['t_ready'], 5 * g + i + 1)
                    for u in range(NU):
                        ins = mm(B[0][:, CH * u:CH * u + CH], LT_bd[:, u, :], T_st[:, u, :])
                    note(ins, 'y_mm')
                    between[i]()
                    pe.wait_ge(S['y_ready'], 5 * g + i + 1)
                    pe.wait_ge(S['tt_ready'], 6 * g + i + 1)
                    if not last:
                        pe.wait_ge(S['ttbd_act'], 6 * g + i + 1)
                        pe.wait_ge(S['ttbd_pool'], 6 * g + i + 1)
                        for u in range(NU):
                            ins = mm(B[2][:, CH * u:CH * u + CH], TT_bd[:, u, :], Y_st[:, u, :])
                        note(ins, 't_mm')
                    pe.wait_ge(S['ybd_act'], 5 * g + i + 1)
                    pe.wait_ge(S['ybd_pool'], 5 * g + i + 1)
                    for u in range(NU):
                        ins = mm(B[3][:, CH * u:CH * u + CH], Y_bd[:, u, :], TT_st[:, u, :])
                    note(ins, 'tt_mm')
                pe.wait_ge(S['ttbd_act'], 6 * g + 6)
                pe.wait_ge(S['ttbd_pool'], 6 * g + 6)
                pe.wait_ge(S['tr_free'], 11 * g + 9)
                pe.wait_ge(S['state_zero'], 2 * (g + 1))
                for c in range(NCH):
                    n = NCH * g + c
                    if c:
                        pe.wait_ge(S['s_ready'], n)
                    for p in range(2):
                        u = NCH * p + c
                        mm(B[0][:, CH * p:CH * p + CH], a_bd[:, u, :], S_st[:, p, :], True, False)
                        ins = mm(B[0][:, CH * p:CH * p + CH], AK_bd[:, u, :], V_st[:, u, :], False, True)
                    note(ins, 'zq_mm')
                    rkv_of_next(g, 4 * c)
                    pe.wait_ge(S['zq_ready'], n + 1)
                    for p in range(2):
                        ins = mm(B[2][:, CH * p:CH * p + CH], TT_bd[:, NCH * p + c, :], Z_st[:, p, :])
                    note(ins, 'u_mm')
                    rkv_of_next(g, 4 * c + 1)
                    pe.wait_ge(S['ust_ready'], n + 1)
                    for p in range(2):
                        u = NCH * p + c
                        mm(B[0][:, 128 + CH * p:128 + CH * p + CH], BT_bd[:, u, :], U_st[:, p, :], True, False)
                        ins = mm(B[0][:, 128 + CH * p:128 + CH * p + CH], KTok_bd[:, u, :], V_st[:, u, :], False, True)
                    note(ins, 's_mm')
                    rkv_of_next(g, 4 * c + 2)
                    pe.wait_ge(S['ubd_ready'], 2 * (n + 1))
                    if c:
                        pe.wait_ge(S['sbd_ready'], 2 * n)
                        pe.wait_ge(S['o_ready'], n)
                    for p in range(2):
                        u = NCH * p + c
                        o = B[3][:, CH * p:CH * p + CH]
                        mm(o, S_bd[:, p, :], AR[:, u, 1, :], True, False)
                        mm(o, U_bd[:, p, :], X1[:, u, 1, :], False, False)
                        ins = mm(o, V_bd[:, u, :], X2[:, u, 1, :], False, True)
                    note(ins, 'o_mm')
                    rkv_of_next(g, 4 * c + 3)
                bank = ring_bank()
                pe.wait_ge(S['sbd_ready'], 2 * NCH * (g + 1))
                for p in range(2):
                    ins = nc.tensor.transpose(bank[:, 128 * p:128 * p + 128], S_bd[:, p, :], ident)
                note(ins, 'tr_mm')
                bank = ring_bank()
                pe.wait_ge(S['os_in'], 16 * (g + 1))
                for p in range(2):
                    ins = nc.tensor.transpose(bank[:, NS * p:NS * p + NS], OR[0:NS, 128 * p:128 * p + 128],
                                              ident[0:NS, 0:NS])
                note(ins, 'tr_mm')
                pe.wait_ge(S['o_ready'], NCH * (g + 1))
                pe.wait_ge(S['tr_free'], 11 * (g + 1))
                for p in range(2):
                    note(mm(B[p][:, 0:NCOL], K['same_head'], O[:, p, :]), 'gm_mm')
                pe.wait_ge(S['bo_in'], g + 1)
                for p in range(2):
                    note(mm(B[4 + p][:, 0:NCOL], K['same_head'], KK[:, p, :]), 'bo_mm')
                if g + 1 < NG:
                    z_tile(z0 + NZ + 6)
                    z_tile(z0 + NZ + 7)
                pe.wait_ge(S['gsq_ready'], g + 1)
                for p in range(2):
                    note(mm(B[2 + p][:, 0:NCOL], K['same_head'], SQ[:, p, :]), 'gv_mm')
                if g + 1 < NG:
                    z_tile(z0 + NZ + 8)
                    z_tile(z0 + NZ + 9)

            pe.wait_ge(S['ma_ready'], NG)
            pe.wait_ge(S['c_ready'], NG)
            for k in range(KT):
                ins = mm(ZP[0][:, 0:NCOL], K['ones'], C[:, k, :], k == 0, k == KT - 1)
            note(ins, 'cm_mm')
            pe.wait_ge(S['csq_ready'], 1)
            for k in range(KT):
                ins = mm(ZP[1][:, 0:NCOL], K['ones'], CS[:, k, :], k == 0, k == KT - 1)
            note(ins, 'cv_mm')
            pe.wait_ge(S['wout_in'], 32)
            for k in range(KT):
                pe.wait_ge(S['merged_ready'], k + 1)
                for t in range(3):
                    lhsT = MA[:, k, 128 * t:128 * t + 128] if t < 2 else MA[:, k, NP + 1:NCOL:2]
                    rows = 128 if t < 2 else NS
                    for h in range(2):
                        ins = mm(B[2 * t + h][0:rows, :], lhsT, w_out_sb[:, k, 512 * h:512 * h + 512],
                                 k == 0, k == KT - 1)
            note(ins, 'wo_mm')
            moe_pe(pe, note, mm)

        @block.scalar
        def _(act):
            note, link = counted(act)

            def fn(out_, in_, f, **kw):
                return nc.scalar.activation(out_, in_, f, **kw)

            act.wait_ge(S['consts_in'], 16)
            act.wait_ge(S['x_in'], 16)
            for t in range(3):
                rows = 128 if t < 2 else NS
                if t == 2:
                    act.wait_ge(S['small_in'], 48)
                link(fn(junk[0:rows, :], xrow[0:rows, t, :], ACT.Square, accum_out=stat[0:rows, t:t + 1]), 'act_chain')
                note(fn(stat[0:rows, 3 + t:4 + t], stat[0:rows, t:t + 1], ACT.Sqrt,
                        scale=1.0 / D, bias=K['rms_eps'][0:rows, :]), 'xstd_ready')
            for i in range(4):
                act.wait_ge(S['xt_mm'], i + 1)
                t, h = i // 2, i % 2
                note(fn(xT[:, 4 * h:4 * h + 4, 128 * t:128 * t + 128],
                        B[i][:, :].rearrange("p (k c) -> p k c", k=4), ACT.Copy), 'xt_ready')
            act.wait_ge(S['xt_mm'], 5)
            b4 = B[4][:, 0:128].rearrange("p (k w s) -> p w k s", k=KT, w=2)
            note(fn(xT[:, :, NP + 1:NCOL:2], b4[:, 0], ACT.Copy), 'xt_ready')
            note(fn(xT[:, :, NP:NCOL:2], b4[:, 1], ACT.Copy), 'xt_ready')
            act.wait_ge(S['vec_mm'], 1)
            note(fn(VC, B[5][:, 0:NVEC], ACT.Copy), 'vec_ready')
            note(fn(CWT.rearrange("p k w -> p (k w)"), B[5][:, 128:128 + KT * CW], ACT.Copy), 'vec_ready')
            act.wait_ge(S['vec_ready'], 1)
            act.wait_ge(S['zero_ready'], 1)
            act.wait_ge(S['bd_zero'], 1)

            def shift_part(n, i):
                act.wait_ge(S['zt_mm'], n + 1)
                note(fn(zs[:, n % 2, 1:NCOL + 1], ZP[n % 2][:, 0:NCOL], ACT.Copy, scale=mucol(i)), 'zs_ready')

            shift_part(0, 24)
            shift_part(1, 25)
            act.wait_ge(S['z_free_dve'], 1)
            note(fn(TW[0:64, :], LZS[1][0:64, 0, 0, :], ACT.Tanh), 'lora_ready')
            note(fn(TW[64:128, :], LZS[1][64:128, 0, 0, :], ACT.Copy), 'lora_ready')
            act.wait_ge(S['z_free_dve'], 2)
            note(fn(SG, LZS[1][:, 0, 1, :], ACT.Sigmoid), 'lora_ready')

            def shift_rkv(g, i):
                shift_part(2 + NZ * g + i, 8 * (i // 2) + 2 * g + i % 2)

            def glu_gate(g, p):
                n = 2 + NZ * g + 6 + p
                act.wait_ge(S['zt_mm'], n + 1)
                note(fn(SB[:, p, :], ZP[n % 2][:, 0:NCOL], ACT.Sigmoid), 'z_free_act')

            for i in range(6):
                shift_rkv(0, i)
            glu_gate(0, 0)
            glu_gate(0, 1)
            ring = [0]

            for g in range(NG):
                z0 = 2 + NZ * g

                def from_ring():
                    i = ring[0]
                    ring[0] += 1
                    act.wait_ge(S['tr_mm'], i + 1)
                    return B[(1, 4, 5)[i % 3]]

                for p in range(2):
                    act.wait_ge(S['lora_mm'], 6 * g + p + 1)
                    note(fn(DC[:, p, :], B[p][:, 0:NCOL], ACT.Sigmoid, bias=vcol('w0', 2 * g + p)), 'lora_free')
                for p in range(2):
                    act.wait_ge(S['lora_mm'], 6 * g + p + 3)
                    note(fn(AA[:, p, :], B[2 + p][:, 0:NCOL], ACT.Sigmoid, bias=vcol('a0', 2 * g + p)), 'lora_free')
                act.wait_ge(S['lora_free'], 6 * g + 2)
                note(fn(DC, DC, ACT.Exp, scale=-EXP_M05), 'dec_ready')
                for p in range(2):
                    act.wait_ge(S['ss_mm'], 2 * g + p + 1)
                    note(fn(INV[:, p, :], B[p][:, 0:NCOL], ACT.Sqrt), 'root_ready')
                for p in range(2):
                    act.wait_ge(S['lora_mm'], 6 * g + p + 5)
                    note(fn(G[:, p, :], B[4 + p][:, 0:NCOL], ACT.Copy), 'lora_free')

                def gate_tile(i):
                    act.wait_ge(S['zt_mm'], z0 + i + 1)
                    dst = GA[:, i - 10, :] if i < 12 else GB[:, 2 * g + i - 12, :]
                    note(fn(dst, ZP[(z0 + i) % 2][:, 0:NCOL], ACT.Sigmoid), 'z_free_act')

                def copy_units(dst, h):
                    b = from_ring()
                    note(fn(dst[:, 4 * h:4 * h + 4, :].rearrange("p u n -> p (u n)"), b[:, :], ACT.Copy), 'tr_free')

                def copy_v(p):
                    b = from_ring()
                    bu = b[:, :].rearrange("p (u n) -> p u n", u=NCH)
                    for lo, hi in halves:
                        nc.scalar.activation(V_bd[lo:hi, NCH * p:NCH * p + NCH, lo:hi], bu[lo:hi, :, lo:hi], ACT.Copy)
                    fn(V_st[0:64, NCH * p:NCH * p + NCH, :], bu[0:64, :, 0:64], ACT.Copy)
                    note(fn(V_st[64:128, NCH * p:NCH * p + NCH, :], bu[64:128, :, 64:128], ACT.Copy), 'tr_free')

                def copy_samples():
                    b = from_ring()
                    wait(act, 'qv_sent', 16 * g)
                    note(fn(QR[0:48, :], b[0:48, 0:256], ACT.Copy), 'tr_free')

                def copy_conv_state():
                    b = from_ring()
                    for p in range(2):
                        ins = fn(SCB[:, p, :, 0:CW - 1],
                                 b[:, 240 * p:240 * p + 240].rearrange("p (s w) -> p s w", s=NS), ACT.Copy)
                    note(ins, 'tr_free')

                def copy_new_conv():
                    b = from_ring()
                    wait(act, 'conv_out', 32 * g)
                    note(fn(UR[0:46, :], b[0:46, 0:256], ACT.Copy), 'tr_free')

                act.wait_ge(S['lora_free'], 6 * g + 4)
                for p in range(2):
                    note(fn(INV2[:, p, :], AA[:, p, :], ACT.Identity, scale=vcol('k_a', 2 * g + p),
                            bias=oka[:, 2 * g + p:2 * g + p + 1]), 'prep_act')
                if g == 0:
                    act.wait_ge(S['z_free_dve'], 8)
                wait(act, 'os_ready', g)
                for p in range(2):
                    note(fn(VD.rearrange("p (a c) r n -> p a c r n", a=2)[:, p],
                            LZS[g % 2][:, 2, p, 0:NP].rearrange("p (c n) -> p c n", n=CH).unsqueeze(2)
                            .broadcast_to([128, NCH, 2, CH]), ACT.Copy), 'prep_act')
                for i in range(10, 14):
                    gate_tile(i)
                act.wait_ge(S['plain_ready'], 4 * g + 2)
                for k, (dst, src) in enumerate(((b_bd, BP), (a_bd, AR[:, :, 0, :]), (k_bd, KP))):
                    if k == 2:
                        act.wait_ge(S['plain_ready'], 4 * g + 3)
                    for lo, hi in halves:
                        note(fn(dst[lo:hi, :, lo:hi], src[lo:hi], ACT.Copy), 'pbd_ready')
                for q, src in enumerate((LZS[g % 2][:, 0], DC, LZS[g % 2][:, 1], LZS[g % 2][:, 2], KK, AA)):
                    note(fn(QS[:, :, q, :], src[:, :, NP + 1:NCOL:2], ACT.Copy), 'qs_ready')
                act.wait_ge(S['lmask_ready'], 4 * g + 2)
                for lo, hi in halves:
                    note(fn(LT_bd[lo:hi, :, lo:hi], X1[lo:hi, :, 0, :], ACT.Copy), 'ltbd_ready')
                evacuate = [
                    lambda: (copy_units(BT_bd, 0), copy_units(BT_bd, 1), copy_samples(), copy_conv_state()),
                    lambda: (copy_units(KTok_bd, 0), copy_units(KTok_bd, 1)),
                    lambda: (copy_v(0), copy_v(1)),
                    lambda: copy_new_conv(),
                    lambda: None,
                ]
                act.wait_ge(S['tt_ready'], 6 * g + 1)
                note(fn(TT_bd[0:64, :, 0:64], TT_st[0:64, :, :], ACT.Copy), 'ttbd_act')
                for i, m in enumerate(LEVELS):
                    evacuate[i]()
                    act.wait_ge(S['y_ready'], 5 * g + i + 1)
                    note(fn(Y_bd[0:64, :, 0:64], Y_st[0:64, :, :], ACT.Copy), 'ybd_act')
                    act.wait_ge(S['tt_ready'], 6 * g + i + 2)
                    note(fn(TT_bd[0:64, :, 0:64], TT_st[0:64, :, :], ACT.Copy), 'ttbd_act')
                for c in range(NCH):
                    n = NCH * g + c
                    act.wait_ge(S['zq_mm'], n + 1)
                    note(fn(Z_st.rearrange("p a n -> p (a n)"), B[0][:, 0:128], ACT.Copy), 'zq_ready')
                    act.wait_ge(S['u_mm'], n + 1)
                    note(fn(U_st.rearrange("p a n -> p (a n)"), B[2][:, 0:128], ACT.Copy), 'ust_ready')
                    if g + 1 < NG:
                        for i in RKV_DONE[c]:
                            shift_rkv(g + 1, i)
                b = from_ring()
                wait(act, 'state_out', 32 * g)
                note(fn(SO.rearrange("p a n -> p (a n)"), b[:, 0:256], ACT.Copy), 'tr_free')
                b = from_ring()
                act.wait_ge(S['o_ready'], NCH * (g + 1))
                note(fn(O[:, :, NP + 1:NCOL:2], b[:, 0:2 * NS].rearrange("p (a s) -> p a s", a=2), ACT.Copy), 'tr_free')
                act.wait_ge(S['gd_ready'], g + 1)
                note(fn(SQ, O, ACT.Square), 'gsq_ready')
                if g + 1 < NG:
                    glu_gate(g + 1, 0)
                for p in range(2):
                    act.wait_ge(S['gv_mm'], 2 * g + p + 1)
                    note(fn(INV[:, p, :], B[2 + p][:, 0:NCOL], ACT.Sqrt, scale=1.0 / CH, bias=K['gn_eps']), 'gstd_ready')
                if g + 1 < NG:
                    glu_gate(g + 1, 1)

            act.wait_ge(S['cd_ready'], 1)
            note(fn(CS, CD, ACT.Square), 'csq_ready')
            act.wait_ge(S['cv_mm'], 1)
            note(fn(lnr, ZP[1][:, 0:NCOL], ACT.Sqrt, scale=1.0 / D, bias=K['ln_eps']), 'cstd_ready')
            for k in range(KT):
                act.wait_ge(S['cn_ready'], k + 1)
                note(fn(CS[:, k, :], CD[:, k, :], ACT.Sigmoid), 'cs_sig')
            moe_act(act, note, link, fn)

        @block.vector
        def _(dve):
            note, link = counted(dve)
            v = nc.vector
            M, AD, SU = ALU.mult, ALU.add, ALU.subtract
            chain = 'dve_chain'

            v.memset(zs[:, :, 0:1], 0.0)
            v.memset(C, 0.0)
            v.memset(UU[:, :, 0:CW - 1], 0.0)
            note(v.memset(PP[:, :, :, 0:1], 1.0), 'zero_ready')

            dve.wait_ge(S['small_in'], 48)
            for t in range(3):
                rows = 128 if t < 2 else NS
                dve.wait_ge(S['xstd_ready'], t + 1)
                link(v.reciprocal(stat[0:rows, 6 + t:7 + t], stat[0:rows, 3 + t:4 + t]), chain)
                link(v.scalar_tensor_tensor(out=xrow[0:rows, t, :], in0=xrow[0:rows, t, :],
                                            scalar=stat[0:rows, 6 + t:7 + t], in1=grow[0:rows, :],
                                            op0=M, op1=M), 'xn_ready')
            dve.wait_ge(S['vec_ready'], 2)
            mu0, ka0 = VOFF['mu_shift'], VOFF['k_a']
            v.tensor_scalar(omu, VC[:, mu0:mu0 + 26], -1.0, 1.0, M, AD)
            link(v.tensor_scalar(oka, VC[:, ka0:ka0 + KT], -1.0, 1.0, M, AD), chain)

            def shifted(n, i, dst):
                dve.wait_ge(S['zs_ready'], (n if n < 2 else 2 + 6 * ((n - 2) // NZ) + (n - 2) % NZ) + 1)
                note(v.scalar_tensor_tensor(out=dst, in0=ZP[n % 2][:, 0:NCOL], scalar=omu[:, i:i + 1],
                                            in1=zs[:, n % 2, 0:NCOL], op0=M, op1=AD), 'z_free_dve')

            def shifted_rkv(g, i):
                shifted(2 + NZ * g + i, 8 * (i // 2) + 2 * g + i % 2, LZS[g % 2][:, i // 2, i % 2, :])

            dve.wait_ge(S['xt_mm'], 5)
            dve.wait_ge(S['shift_out'], 48)
            shifted(0, 24, LZS[1][:, 0, 0, :])
            shifted(1, 25, LZS[1][:, 0, 1, :])
            for i in range(6):
                shifted_rkv(0, i)

            for g in range(NG):
                z0 = 2 + NZ * g
                zf = 2 + 8 * g
                col = lambda name, p: vcol(name, 2 * g + p)
                tok = lambda x: x[:, :, 0:NP].rearrange("p a (c n) -> p a c n", n=CH)
                unit = lambda x: x.rearrange("p (a c) n -> p a c n", a=2)
                dve.wait_ge(S['z_free_dve'], zf + 6)
                LZ = LZS[g % 2]
                R_, K_, V_ = LZ[:, 0], LZ[:, 1], LZ[:, 2]
                for p in range(2):
                    link(v.tensor_scalar(KK[:, p, :], K_[:, p, :], col('k_k', p), None, M), chain)
                link(v.tensor_tensor(SQ, KK, KK, M), 'sq_ready')
                for p in range(2):
                    n = z0 + 8 + p
                    dve.wait_ge(S['z_free_act'], 6 * g + p + 1)
                    dve.wait_ge(S['zt_mm'], n + 1)
                    if p == 0:
                        wait(dve, 'tr_free', 11 * g)
                    link(v.tensor_tensor(UU[:, p, CW - 1:CW - 1 + NCOL], ZP[n % 2][:, 0:NCOL], SB[:, p, :], M),
                         'z_free_dve')
                link(v.tensor_copy(SCB[:, :, :, CW - 1], UU[:, :, CW - 1 + NP + 1:CW - 1 + NCOL:2]), chain)
                dve.wait_ge(S['dec_ready'], g + 1)
                for p in range(2):
                    for c in range(NCH):
                        ins = v.tensor_tensor_scan(PP[:, p, c, 1:CH + 1], DC[:, p, CH * c:CH * c + CH],
                                                   K['ones'][:, 0:CH], 1.0, M, M)
                        (note if (p, c) != (1, NCH - 1) else link)(ins, chain)
                link(v.reciprocal(IP, PP[:, :, :, 1:CH + 1]), chain)
                dve.wait_ge(S['prep_act'], 4 * g + 2)
                link(v.tensor_tensor(K_, K_, INV2, M), chain)
                dve.wait_ge(S['root_ready'], 2 * (g + 1))
                link(v.tensor_scalar(INV, INV, 1e-12, None, ALU.max), chain)
                link(v.reciprocal(INV, INV), chain)
                link(v.tensor_tensor(KK, KK, INV, M), chain)
                link(v.tensor_tensor(AA, KK, AA, M), chain)
                prev, cur = PP[:, :, :, 0:CH], PP[:, :, :, 1:CH + 1]
                for p in range(2):
                    u4 = slice(NCH * p, NCH * p + NCH)
                    ins = v.scalar_tensor_tensor(out=AR[:, u4, 0, :], in0=tok(KK)[:, p], scalar=-1.0,
                                                 in1=prev[:, p], op0=M, op1=M)
                note(ins, 'plain_ready')
                note(v.tensor_tensor(unit(BP), tok(AA), IP, M), 'plain_ready')
                note(v.tensor_tensor(unit(KP), tok(K_), IP, M), 'plain_ready')
                for p in range(2):
                    u4 = slice(NCH * p, NCH * p + NCH)
                    ins = v.tensor_tensor(AR[:, u4, 1, :], tok(R_)[:, p], cur[:, p], M)
                link(ins, 'plain_ready')
                def taps():
                    for w in range(CW):
                        for p in range(2):
                            acc, u = C[:, 2 * g + p, 0:NP], UU[:, p, w:w + NP]
                            cw = CWT[:, 2 * g + p, w:w + 1]
                            if w:
                                dve.wait_ge(S['tap'], 62 * g + 2 * w + p - 1)
                            if w == 0:
                                note(v.tensor_scalar(acc, u, cw, col('conv_b', p), M, AD), 'tap')
                            else:
                                note(v.scalar_tensor_tensor(out=acc, in0=u, scalar=cw, in1=acc, op0=M, op1=AD), 'tap')
                            yield

                tap = taps()

                def some_taps(n):
                    for _ in range(n):
                        next(tap, None)

                some_taps(16)
                up = K['upper'].rearrange("p (w n) -> p w n", w=2)
                for h in range(2):
                    dve.wait_ge(S['a_mm'], 5 * g + h + 1)
                    note(v.tensor_tensor(X1[:, 4 * h:4 * h + 4],
                                         B[2 + h][:, :].rearrange("p (u w n) -> p u w n", u=4, w=2),
                                         up.unsqueeze(1).broadcast_to([128, 4, 2, CH]), M), 'lmask_ready')
                dve.wait_ge(S['lmask_ready'], 4 * g + 2)
                bc = lambda k: K[k].unsqueeze(1).broadcast_to([128, NU, CH])
                bank = lambda i: B[i][:, :].rearrange("p (u n) -> p u n", u=NU)
                dve.wait_ge(S['a_mm'], 5 * g + 3)
                link(v.tensor_tensor(T_st, bank(0), bc('pair_low'), M), chain)
                link(v.tensor_tensor(T_st, T_st, bc('eye_st'), AD), 't_ready')
                link(v.tensor_tensor(TT_st, X1[:, :, 0, :], bc('pair_up'), M), chain)
                link(v.tensor_tensor(TT_st, TT_st, bc('eye_st'), AD), 'tt_ready')
                for h in range(2):
                    dve.wait_ge(S['a_mm'], 5 * g + h + 4)
                    note(v.tensor_tensor(X2[:, 4 * h:4 * h + 4],
                                         B[4 + h][:, :].rearrange("p (u w n) -> p u w n", u=4, w=2),
                                         up.unsqueeze(1).broadcast_to([128, 4, 2, CH]), M), 'lmask_ready')

                for i, m in enumerate(LEVELS):
                    some_taps(2)
                    dve.wait_ge(S['y_mm'], 5 * g + i + 1)
                    wait(dve, 'tt_mm', 5 * g + i)
                    link(v.tensor_tensor(Y_st, bank(0), bc(f'level{m}'), M), 'y_ready')
                    some_taps(4)
                    if i < len(LEVELS) - 1:
                        dve.wait_ge(S['t_mm'], 4 * g + i + 1)
                        link(v.tensor_tensor(T_st, T_st, bank(2), AD), 't_ready')
                    dve.wait_ge(S['tt_mm'], 5 * g + i + 1)
                    dve.wait_ge(S['ttbd_act'], 6 * g + i + 1)
                    dve.wait_ge(S['ttbd_pool'], 6 * g + i + 1)
                    link(v.tensor_tensor(TT_st, TT_st, bank(3), AD), 'tt_ready')

                qk = lambda q: QV[:, q, :].unsqueeze(1).broadcast_to([128, 16, CH])
                row = lambda x: x.unsqueeze(2).broadcast_to([128, 16, CH])

                def sample_part(c):
                    if c == 0:
                        dve.wait_ge(S['qv_in'], 16 * 5 * (g + 1))
                        dve.wait_ge(S['sst_in'], 16 * 8 * (g + 1))
                        link(v.tensor_tensor(SMT, SM, qk(4), M), chain)
                        link(v.tensor_reduce(SA, SMT, AX.X, AD), chain)
                        link(v.tensor_tensor(SM, SM, qk(1), M), chain)
                    elif c == 1:
                        link(v.tensor_tensor(SMT, row(SA), qk(5), M), chain)
                        link(v.tensor_tensor(SM, SM, SMT, SU), chain)
                    elif c == 2:
                        link(v.tensor_tensor(SMT, row(QVV), qk(2), M), chain)
                        link(v.tensor_tensor(SM, SM, SMT, AD), 'sm_ready')
                    else:
                        link(v.tensor_tensor(SMT, SM, qk(0), M), chain)
                        link(v.tensor_reduce(OS, SMT, AX.X, AD), 'os_ready')

                wait(dve, 's_mm', NCH * g)
                wait(dve, 'o_mm', NCH * g)
                wait(dve, 'sbd_ready', 2 * NCH * g)
                if g == 0:
                    dve.wait_ge(S['bd_zero'], 1)
                wait(dve, 'tr_free', 11 * g)
                v.memset(S_st, 0.0)
                note(v.memset(S_bd[0:64, :, 0:64], 0.0), 'state_zero')
                note(v.memset(S_bd[64:128, :, 64:128], 0.0), 'state_zero')
                dve.wait_ge(S['state_zero'], 2 * (g + 1))
                for c in range(NCH):
                    n = NCH * g + c
                    some_taps(4)
                    if c < 3:
                        sample_part(c)
                    if c == 2:
                        sample_part(3)
                    dve.wait_ge(S['s_mm'], n + 1)
                    if c:
                        dve.wait_ge(S['sbd_ready'], 2 * n)
                    link(v.tensor_tensor(S_st, S_st, B[0][:, 128:256].rearrange("p (a n) -> p a n", a=2), AD), chain)
                    for p in range(2):
                        ins = v.tensor_scalar(S_st[:, p, :], S_st[:, p, :], PP[:, p, c, CH:CH + 1], None, M)
                        if p == 0:
                            note(ins, chain)
                    link(ins, 's_ready')
                    dve.wait_ge(S['o_mm'], n + 1)
                    link(v.tensor_copy(O[:, :, CH * c:CH * c + CH], B[3][:, 0:128].rearrange("p (a n) -> p a n", a=2)),
                         'o_ready')
                    if g + 1 < NG:
                        if c == 0 and g == 0:
                            dve.wait_ge(S['lora_ready'], 3)
                        for i in RKV_DONE[c]:
                            shifted_rkv(g + 1, i)
                link(v.tensor_tensor(KK, R_, K_, M), chain)
                for p in range(2):
                    ins = v.tensor_scalar(KK[:, p, :], KK[:, p, :], col('r_k', p), None, M)
                    if p == 0:
                        link(ins, chain)
                link(ins, 'bo_in')
                for p in range(2):
                    dve.wait_ge(S['gm_mm'], 2 * g + p + 1)
                    ins = v.scalar_tensor_tensor(out=O[:, p, :], in0=B[p][:, 0:NCOL], scalar=-1.0 / CH,
                                                 in1=O[:, p, :], op0=M, op1=AD)
                    if p == 0:
                        link(ins, chain)
                link(ins, 'gd_ready')
                some_taps(62)
                for p in range(2):
                    link(v.tensor_tensor(SCT, SCB[:, p], CWT[:, 2 * g + p].unsqueeze(1).broadcast_to([128, NS, CW]), M),
                         chain)
                    link(v.tensor_reduce(SCR8, SCT, AX.X, AD), chain)
                    link(v.tensor_scalar(C[:, 2 * g + p, NP + 1:NCOL:2], SCR8, col('conv_b', p), None, AD), chain)
                dve.wait_ge(S['tap'], 62 * (g + 1))
                note(v.memset(zero1, 0.0), 'c_ready')
                dve.wait_ge(S['gstd_ready'], 2 * (g + 1))
                link(v.reciprocal(INV, INV), chain)
                link(v.tensor_tensor(O, O, INV, M), chain)
                for p in range(2):
                    link(v.tensor_scalar(O[:, p, :], O[:, p, :], col('gn_g', p), col('gn_b', p), M, AD), chain)
                for p in range(2):
                    dve.wait_ge(S['bo_mm'], 2 * g + p + 1)
                    link(v.tensor_tensor(INV[:, p, :], B[4 + p][:, 0:NCOL], V_[:, p, :], M), chain)
                link(v.tensor_tensor(O, O, INV, AD), chain)
                link(v.tensor_tensor(O, O, G, M), chain)
                dve.wait_ge(S['z_free_act'], 6 * g + 6)
                link(v.tensor_tensor(MA[:, 2 * g:2 * g + 2, :], O, GA, M), 'ma_ready')

            dve.wait_ge(S['cm_mm'], 1)
            link(v.scalar_tensor_tensor(out=CD, in0=ZP[0][:, 0:NCOL].unsqueeze(1).broadcast_to([128, KT, NCOL]),
                                        scalar=-1.0 / D, in1=C, op0=M, op1=AD), 'cd_ready')
            dve.wait_ge(S['cstd_ready'], 1)
            link(v.reciprocal(lnr, lnr), chain)
            dve.wait_ge(S['csq_ready'], 1)
            link(v.tensor_tensor(CD, CD, lnr.unsqueeze(1).broadcast_to([128, KT, NCOL]), M), chain)
            dve.wait_ge(S['cv_mm'], 1)
            for k in range(KT):
                note(v.tensor_scalar(CD[:, k, :], CD[:, k, :], vcol('cln_g', k), vcol('cln_b', k), M, AD), 'cn_ready')
            for k in range(KT):
                dve.wait_ge(S['cs_sig'], k + 1)
                link(v.tensor_tensor(CD[:, k, :], CD[:, k, :], CS[:, k, :], M), chain)
                link(v.tensor_tensor(CD[:, k, :], CD[:, k, :], GB[:, k, :], M), chain)
                link(v.tensor_tensor(MA[:, k, :], MA[:, k, :], CD[:, k, :], AD), 'merged_ready')
            moe_dve(dve, note, link, v)

        @block.gpsimd
        def _(pool):
            note, link = counted(pool)
            gp = nc.gpsimd
            for x in (a_bd, b_bd, k_bd, LT_bd, AK_bd, TT_bd, Y_bd, V_bd, U_bd):
                gp.memset(x, 0.0)
            link(gp.memset(S_bd, 0.0), 'bd_zero')
            pool.wait_ge(S['xn_ready'], 3)
            pool.dma_start(out['shift_p'][0], xrow[127:128, 1, :]).then_inc(S['shift_out'], 16)
            pool.dma_start(out['shift_s'][0], xrow[0:NS, 2, :]).then_inc(S['shift_out'], 16)
            pool.dma_start(out['conv_s'][0][:, 0:CW - 2, :], A['state_conv'][0][:, 1:CW - 1, :]) \
                .then_inc(S['shift_out'], 16)

            for g in range(NG):
                pool.wait_ge(S['tt_ready'], 6 * g + 1)
                link(gp.tensor_copy(TT_bd[64:128, :, 64:128], TT_st[64:128, :, :]), 'ttbd_pool')
                pool.wait_ge(S['lmask_ready'], 4 * g + 4)
                for lo, hi in halves:
                    link(gp.tensor_copy(AK_bd[lo:hi, :, lo:hi], X2[lo:hi, :, 0, :]), 'lbd_ready')
                for i in range(len(LEVELS)):
                    pool.wait_ge(S['y_ready'], 5 * g + i + 1)
                    link(gp.tensor_copy(Y_bd[64:128, :, 64:128], Y_st[64:128, :, :]), 'ybd_pool')
                    pool.wait_ge(S['tt_ready'], 6 * g + i + 2)
                    link(gp.tensor_copy(TT_bd[64:128, :, 64:128], TT_st[64:128, :, :]), 'ttbd_pool')
                for c in range(NCH):
                    n = NCH * g + c
                    pool.wait_ge(S['ust_ready'], n + 1)
                    for lo, hi in halves:
                        link(gp.tensor_copy(U_bd[lo:hi, :, lo:hi], U_st[lo:hi]), 'ubd_ready')
                    pool.wait_ge(S['s_ready'], n + 1)
                    pool.wait_ge(S['o_mm'], n + 1)
                    for lo, hi in halves:
                        link(gp.tensor_copy(S_bd[lo:hi, :, lo:hi], S_st[lo:hi]), 'sbd_ready')
            pool.wait_ge(S['shift_out'], 48)
            moe_pool(pool)

_INS = ['x_prompt', 'x_sample', 'state_wkv', 'state_shift', 'state_conv', 'norm1_g', 'w_in', 'mu_shift', 'w0',
        'w_decay_up', 'a0', 'a_up', 'g_up', 'k_k', 'k_a', 'r_k', 'gn_g', 'gn_b', 'conv_w', 'conv_b', 'cln_g',
        'cln_b', 'w_out', 'norm2_g', 'w_router', 'e_bias', 'w_gate', 'w_up', 'w_down', 'ws_gate', 'ws_up',
        'ws_down', 'normf_g']
_OUTS = [('y_p', (1, NP, D)), ('y_s', (NS, 1, D)), ('wkv_p', (1, 1, 16, CH, CH)), ('shift_p', (1, 1, D)),
         ('conv_p', (1, 1, CW - 1, D)), ('wkv_s', (1, NS, 16, CH, CH)), ('shift_s', (1, NS, D)),
         ('conv_s', (1, NS, CW - 1, D))]


def kernel(**inputs):
    import concourse.bacc as _bacc
    from concourse.bass_utils import run_bass_kernel_spmd as _run

    nc = _bacc.Bacc("TRN2", target_bir_lowering=False, num_devices=1)
    arrays = {f"in_{n}": np.ascontiguousarray(inputs[n]) for n in _INS}
    arrays["in_const"] = CONST_ARRAY
    A = {n[3:]: nc.dram_tensor(n, a.shape, F32, kind="ExternalInput").ap() for n, a in arrays.items()}
    out = {n: nc.dram_tensor(f"out_{n}", shape, F32, kind="ExternalOutput").ap() for n, shape in _OUTS}
    layer_step(nc, A, out)
    r = _run(nc, [arrays], core_ids=[0])
    return tuple(r.results[0][f"out_{n}"] for n, _ in _OUTS)
```
